# Optimizing a Trainium2 kernel written in Bass

```python
import math
import jax, jax.numpy as jnp
from jax import lax
import numpy as np

D_MODEL = 1024
BATCH = 1
SEQ = 512
DEPTH = 1

CHUNK = 64
D_MIX = 2 * D_MODEL
D_SSM = D_MIX // 2
D_CONV = D_MIX - D_SSM
SSM_HEAD_DIM = 64
SSM_HEADS = D_SSM // SSM_HEAD_DIM
SSM_GROUPS = 2
SSM_STATE = 128
SSM_CONV_W = 4
SSM_XBC = D_SSM + 2 * SSM_GROUPS * SSM_STATE
CONF_KERNEL = 31
D_FF = 2816
D_IN_PROJ = D_SSM + SSM_XBC + SSM_HEADS + 2 * D_CONV
EPS = 1e-6

kernel_name = 'hybrid_ssd_conformer_conv_macaron_block'

def rms_norm(x, g):
    xf = x.astype(jnp.float32)
    y = xf * lax.rsqrt(jnp.mean(xf * xf, axis=-1, keepdims=True) + EPS)
    return (y * g.astype(jnp.float32)).astype(x.dtype)

def layer_norm(x, g, b):
    xf = x.astype(jnp.float32)
    mu = jnp.mean(xf, axis=-1, keepdims=True)
    var = jnp.mean(jnp.square(xf - mu), axis=-1, keepdims=True)
    y = (xf - mu) * lax.rsqrt(var + EPS)
    return (y * g.astype(jnp.float32) + b.astype(jnp.float32)).astype(x.dtype)

def causal_depthwise_conv(x, w, b):
    k = w.shape[0]
    y = lax.conv_general_dilated(
        x, w[:, None, :], window_strides=(1,), padding=[(k - 1, 0)],
        dimension_numbers=('NWC', 'WIO', 'NWC'), feature_group_count=x.shape[-1])
    return y + b

def swiglu(h, w_gate, w_up, w_down):
    return (jax.nn.silu(h @ w_gate) * (h @ w_up)) @ w_down

def ssd_chunked(xh, dt, a, bm, cm):
    b, seq = xh.shape[:2]
    nc = seq // CHUNK
    g, r, p, n = SSM_GROUPS, SSM_HEADS // SSM_GROUPS, SSM_HEAD_DIM, SSM_STATE
    f32 = jnp.float32
    xc = (xh.astype(f32) * dt[..., None]).reshape(b, nc, CHUNK, g, r, p)
    bc = bm.astype(f32).reshape(b, nc, CHUNK, g, n)
    cc = cm.astype(f32).reshape(b, nc, CHUNK, g, n)
    da = (dt * a).reshape(b, nc, CHUNK, g, r).transpose(0, 1, 3, 4, 2)
    a_cs = jnp.cumsum(da, axis=-1)
    causal = jnp.tril(jnp.ones((CHUNK, CHUNK), dtype=bool))
    seg = a_cs[..., :, None] - a_cs[..., None, :]
    decay_ls = jnp.exp(jnp.where(causal, seg, -jnp.inf))
    cb = jnp.einsum('bclgn,bcsgn->bcgls', cc, bc)
    y_diag = jnp.einsum('bcgls,bcgrls,bcsgrp->bclgrp', cb, decay_ls, xc)
    decay_to_end = jnp.exp(a_cs[..., -1:] - a_cs)
    states = jnp.einsum('bclgn,bcgrl,bclgrp->bcgrpn', bc, decay_to_end, xc)
    chunk_decay = jnp.exp(a_cs[..., -1])

    def step(h, inp):
        s, d = inp
        return h * d[..., None, None] + s, h

    h0 = jnp.zeros((b, g, r, p, n), f32)
    _, prev = lax.scan(step, h0, (jnp.swapaxes(states, 0, 1), jnp.swapaxes(chunk_decay, 0, 1)))
    prev = jnp.swapaxes(prev, 0, 1)
    y_off = jnp.einsum('bclgn,bcgrpn,bcgrl->bclgrp', cc, prev, jnp.exp(a_cs))
    return (y_diag + y_off).reshape(b, seq, SSM_HEADS, p)

def hybrid_mixer(h, w_in, b_glu, ssd_conv_w, ssd_conv_b, dt_bias, a_log, d_skip, ssd_norm_g,
                 conf_dw_w, conf_dw_b, conf_ln_g, conf_ln_b, w_out):
    b, seq, _ = h.shape
    f32 = jnp.float32
    proj = h @ w_in
    z, xbc, dt_raw, glu = jnp.split(
        proj, [D_SSM, D_SSM + SSM_XBC, D_SSM + SSM_XBC + SSM_HEADS], axis=-1)
    xbc = jax.nn.silu(causal_depthwise_conv(xbc, ssd_conv_w, ssd_conv_b))
    xs, bm, cm = jnp.split(xbc, [D_SSM, D_SSM + SSM_GROUPS * SSM_STATE], axis=-1)
    dt = jax.nn.softplus(dt_raw.astype(f32) + dt_bias.astype(f32))
    a = -jnp.exp(a_log.astype(f32))
    xh = xs.reshape(b, seq, SSM_HEADS, SSM_HEAD_DIM)
    y = ssd_chunked(xh, dt, a,
                    bm.reshape(b, seq, SSM_GROUPS, SSM_STATE),
                    cm.reshape(b, seq, SSM_GROUPS, SSM_STATE))
    y = y + d_skip.astype(f32)[:, None] * xh.astype(f32)
    y = y.reshape(b, seq, D_SSM) * jax.nn.silu(z.astype(f32))
    yg = y.reshape(b, seq, SSM_GROUPS, D_SSM // SSM_GROUPS)
    yg = yg * lax.rsqrt(jnp.mean(yg * yg, axis=-1, keepdims=True) + EPS)
    y_ssd = (yg.reshape(b, seq, D_SSM) * ssd_norm_g.astype(f32)).astype(h.dtype)
    u_a, u_g = jnp.split(glu + b_glu, 2, axis=-1)
    u = u_a * jax.nn.sigmoid(u_g)
    u = causal_depthwise_conv(u, conf_dw_w, conf_dw_b)
    y_conv = jax.nn.silu(layer_norm(u, conf_ln_g, conf_ln_b))
    return jnp.concatenate([y_ssd, y_conv], axis=-1) @ w_out

def setup_inputs(seed: int = 0) -> dict:
    key = jax.random.key(seed)
    ks = jax.random.split(key, 32)
    f32 = jnp.float32

    def nrm(k, shape, scale):
        return jax.random.normal(k, shape, f32) * scale

    def gain(k, shape):
        return 1.0 + 0.05 * jax.random.normal(k, shape, f32)

    L = DEPTH
    dt0 = jnp.exp(jax.random.uniform(ks[10], (L, SSM_HEADS), f32)
                  * (math.log(0.1) - math.log(0.001)) + math.log(0.001))
    return {
        'x': jax.random.normal(ks[0], (BATCH, SEQ, D_MODEL), f32),
        'ffn1_pre_g': gain(ks[1], (L, D_MODEL)),
        'ffn1_w_gate': nrm(ks[2], (L, D_MODEL, D_FF), D_MODEL ** -0.5),
        'ffn1_w_up': nrm(ks[3], (L, D_MODEL, D_FF), D_MODEL ** -0.5),
        'ffn1_w_down': nrm(ks[4], (L, D_FF, D_MODEL), D_FF ** -0.5),
        'ffn1_post_g': gain(ks[5], (L, D_MODEL)),
        'mix_pre_g': gain(ks[6], (L, D_MODEL)),
        'w_in': nrm(ks[7], (L, D_MODEL, D_IN_PROJ), D_MODEL ** -0.5),
        'b_glu': nrm(ks[8], (L, 2 * D_CONV), 0.01),
        'ssd_conv_w': nrm(ks[9], (L, SSM_CONV_W, SSM_XBC), SSM_CONV_W ** -0.5),
        'ssd_conv_b': nrm(ks[11], (L, SSM_XBC), 0.01),
        'dt_bias': dt0 + jnp.log(-jnp.expm1(-dt0)),
        'a_log': jnp.log(jax.random.uniform(ks[12], (L, SSM_HEADS), f32, 1.0, 16.0)),
        'd_skip': 1.0 + 0.1 * jax.random.normal(ks[13], (L, SSM_HEADS), f32),
        'ssd_norm_g': gain(ks[14], (L, D_SSM)),
        'conf_dw_w': nrm(ks[15], (L, CONF_KERNEL, D_CONV), CONF_KERNEL ** -0.5),
        'conf_dw_b': nrm(ks[16], (L, D_CONV), 0.01),
        'conf_ln_g': gain(ks[17], (L, D_CONV)),
        'conf_ln_b': nrm(ks[18], (L, D_CONV), 0.01),
        'w_out': nrm(ks[19], (L, D_MIX, D_MODEL), D_MIX ** -0.5),
        'mix_post_g': gain(ks[20], (L, D_MODEL)),
        'ffn2_pre_g': gain(ks[21], (L, D_MODEL)),
        'ffn2_w_gate': nrm(ks[22], (L, D_MODEL, D_FF), D_MODEL ** -0.5),
        'ffn2_w_up': nrm(ks[23], (L, D_MODEL, D_FF), D_MODEL ** -0.5),
        'ffn2_w_down': nrm(ks[24], (L, D_FF, D_MODEL), D_FF ** -0.5),
        'ffn2_post_g': gain(ks[25], (L, D_MODEL)),
    }

def reference(x, ffn1_pre_g, ffn1_w_gate, ffn1_w_up, ffn1_w_down, ffn1_post_g,
              mix_pre_g, w_in, b_glu, ssd_conv_w, ssd_conv_b, dt_bias, a_log, d_skip,
              ssd_norm_g, conf_dw_w, conf_dw_b, conf_ln_g, conf_ln_b, w_out, mix_post_g,
              ffn2_pre_g, ffn2_w_gate, ffn2_w_up, ffn2_w_down, ffn2_post_g):
    for i in range(DEPTH):
        f = swiglu(rms_norm(x, ffn1_pre_g[i]), ffn1_w_gate[i], ffn1_w_up[i], ffn1_w_down[i])
        x = x + 0.5 * rms_norm(f, ffn1_post_g[i])
        m = hybrid_mixer(rms_norm(x, mix_pre_g[i]), w_in[i], b_glu[i], ssd_conv_w[i],
                         ssd_conv_b[i], dt_bias[i], a_log[i], d_skip[i], ssd_norm_g[i],
                         conf_dw_w[i], conf_dw_b[i], conf_ln_g[i], conf_ln_b[i], w_out[i])
        x = x + rms_norm(m, mix_post_g[i])
        f = swiglu(rms_norm(x, ffn2_pre_g[i]), ffn2_w_gate[i], ffn2_w_up[i], ffn2_w_down[i])
        x = x + 0.5 * rms_norm(f, ffn2_post_g[i])
    return x


_drawn_inputs = setup_inputs


def setup_inputs(seed=0):
    import zlib

    import numpy as np

    out = dict(_drawn_inputs(seed))
    spreads = {}
    factors = {'b_glu': 8.0,
     'ssd_conv_b': 6.862,
     'conf_dw_b': 7.764,
     'conf_ln_b': 8.0,
     'ffn2_post_g': 3.541}
    for name, (base, spread) in spreads.items():
        noise = np.random.default_rng([zlib.crc32(name.encode()), seed]).standard_normal(out[name].shape)
        drawn = base * np.exp(spread * noise) if base else spread * noise
        out[name] = __import__('jax').numpy.asarray(drawn.astype(out[name].dtype))
    for name, factor in factors.items():
        out[name] = (out[name] * factor).astype(out[name].dtype)
    return out
```

```python
from contextlib import ExitStack

import concourse.bass as bass
from concourse import mybir

ALU = mybir.AluOpType
ACT = mybir.ActivationFunctionType
F32 = mybir.dt.float32
F32R = mybir.dt.float32r

P = 128
T = 512
D = 1024
FF = 2816
DK = D // P
FK = FF // P
KH = FK // 2
CW = 256
D_SSM = 1024
STATE = 128
GROUPS = 2
HEADS = 16
HD = 64
XBC = D_SSM + 2 * GROUPS * STATE
XT = XBC // P
D_CONV = 1024
TAPS = 31
STAPS = 4
SC = T // P
HG = HEADS // GROUPS
EPS = 1e-6

Z0 = 0
XBC0 = D_SSM
DT0 = XBC0 + XBC
GLU0 = DT0 + HEADS

IT_GU1 = 0
IT_DOWN1 = IT_GU1 + FK // 2
IT_GLU = IT_DOWN1 + DK // 2
IT_XBC = IT_GLU + DK // 2
IT_Z = IT_XBC + XT // 4
IT_OUT = IT_Z + DK // 4
IT_GU2 = IT_OUT + DK // 2
IT_DOWN2 = IT_GU2 + FK // 2
IT_END = IT_DOWN2 + DK // 2
PR_GU1 = 0
PR_GLU = FK // 2
PR_XBC = PR_GLU + DK // 2
PR_Z = PR_XBC + XT // 4
PR_GU2 = PR_Z + DK // 4
AC_DOWN1 = 0
AC_OUT = DK // 2
AC_DOWN2 = DK

VECS = [("ffn1_pre_g", 8), ("ffn1_post_g", 8), ("mix_pre_g", 8), ("mix_post_g", 8), ("ffn2_pre_g", 8),
        ("ffn2_post_g", 8), ("ssd_norm_g", 8), ("conf_ln_g", 8), ("conf_ln_b", 8), ("conf_dw_b", 8),
        ("b_glu", 16), ("ssd_conv_b", 12)]
COL = {}
_at = 0
for _n, _k in VECS:
    COL[_n] = _at
    _at += _k
NVEC = _at
COL["ssd_conv_w"] = NVEC
COL["conf_dw_w"] = NVEC + STAPS * XT
HALF_ROWS = TAPS * DK // 2
NPAR = NVEC + STAPS * XT + TAPS * DK


CONV_PAIRS = DK // 2
CONV_PLAN = [12, 13, 13, 13, 8, 8, 8, 12, 12, CONV_PAIRS * (TAPS - 1) - 99]


def conv_segments():
    steps = [(q, s) for q in range(CONV_PAIRS) for s in range(1, TAPS)]
    at, out = 0, []
    for n in CONV_PLAN:
        out.append(steps[at:at + n])
        at += n
    assert at == len(steps)
    return out


def build(nc, a, out):
    ctx = ExitStack()
    with ctx:
        def sem(name):
            return ctx.enter_context(nc.semaphore(name))

        top = [(nc.sbuf_base + 63) // 64 * 64]

        def region(size):
            at = top[0]
            top[0] += (size + 31) // 32 * 32
            assert top[0] <= nc.sbuf_usable_end, (top[0], nc.sbuf_usable_end)
            return at

        def at(name, shape, dt, offset):
            return nc.alloc_sbuf_tensor_at(name, shape, dt, offset=offset)

        WB = KH * CW * 4
        TB = T * 4
        w_raw = [at(f"w_raw{s}", [P, KH * CW], F32, region(WB)) for s in range(2)]
        hi_at = [region(WB) for _ in range(2)]
        lo_at = [region(WB) for _ in range(2)]
        w_hi = [at(f"w_hi{s}", [P, KH * CW], F32R, hi_at[s]) for s in range(2)]
        w_lo = [at(f"w_lo{s}", [P, KH * CW], F32R, lo_at[s]) for s in range(2)]

        X_AT, XH_AT, XL_AT = region(DK * TB), region(DK * TB), region(DK * TB)
        x = at("x_res", [P, DK, T], F32, X_AT)
        xh = at("xh", [P, DK, T], F32R, XH_AT)
        xl = at("xl", [P, DK, T], F32R, XL_AT)
        xv = at("xv", [P, DK, T], F32, XL_AT)
        fo = at("fo", [P, DK, T], F32, XH_AT)
        sq_norm = at("sq_norm", [P, T], F32, XL_AT)

        HB = region(2 * FK * TB)

        def slot(name, s, shape, dt):
            return at(name, shape, dt, HB + s * TB)

        hh = slot("hh", 0, [P, FK, T], F32R)
        hl = slot("hl", FK, [P, FK, T], F32R)
        hs = slot("hs", FK, [P, FK, T], F32)
        x_tok = slot("x_tok", 0, [P, SC, D], F32)
        par_rows = slot("par_rows", 8, [P, 4, P], F32)
        u = slot("u", 0, [P, DK, T], F32)
        xbc = slot("xbc", 8, [P, XT, T], F32)
        z = slot("z", 20, [P, DK, T], F32)
        x_dt = slot("x_dt", 28, [P, SC, D_SSM], F32)
        b_tok = slot("b_tok", 36, [P, GROUPS, SC, STATE], F32)
        g_mask = slot("g_mask", 38, [P, GROUPS, SC, P], F32)
        sg = slot("sg", 40, [P, 2, T], F32)
        dtw = slot("dtw", 42, [P, DK, HEADS], F32)
        dtwh = at("dtwh", [P, DK, HEADS], F32R, HB + 42 * TB + 512)
        dtwl = at("dtwl", [P, DK, HEADS], F32R, HB + 42 * TB + 1024)
        sq_ssd = slot("sq_ssd", 40, [P, GROUPS, T], F32)
        sq_ln = slot("sq_ln", 42, [P, T], F32)
        hst = at("hst", [P, SC - 1, D_SSM], F32, XH_AT)
        x_dec = at("x_dec", [P, 2, T], F32, XH_AT + 6 * TB)
        l_t = at("l_t", [P, 2, T], F32, XL_AT)
        e_t = at("e_t", [P, 2, T], F32, XL_AT + 2 * TB)
        m_t = at("m_t", [P, 2, T], F32, XL_AT + 4 * TB)
        ysh = slot("ysh", 8, [P, DK, T], F32R)
        ysl = slot("ysl", 20, [P, DK, T], F32R)
        ych = slot("ych", 28, [P, DK, T], F32R)
        ycl = slot("ycl", 0, [P, DK, T], F32R)

        def small(name, shape):
            n = 4
            for d in shape[1:]:
                n *= d
            return at(name, shape, F32, region(n))

        par = small("par", [P, NPAR])
        ones = small("ones", [P, P])
        tri = small("tri", [P, P])
        ident = small("ident", [P, P])
        d_col = small("d_col", [P, DK])
        eps = small("eps", [P, 1])
        spare = small("spare", [P, 2])
        dtb = small("dtb", [P, HEADS])
        alog = small("alog", [P, HEADS])
        dt_tok = small("dt_tok", [P, SC, HEADS])
        da_tok = small("da_tok", [P, SC, HEADS])
        t_abs = small("t_abs", [P, SC, HEADS])
        acs = small("acs", [P, SC, HEADS])
        dend = small("dend", [P, SC, HEADS])
        wdec = small("wdec", [P, SC, HEADS])

        bank = [nc.alloc_psum_tensor(f"bank{b}", [P, T], F32) for b in range(8)]

        def col(name, k):
            c = COL[name] + k
            return par[:, c:c + 1]

        raw_in = [sem(f"raw_in{s}") for s in range(2)]
        hi_done = sem("hi_done")
        lo_done = sem("lo_done")
        w_used = sem("w_used")
        x_in = [sem(f"x_in{c}") for c in range(SC)]
        par_in = sem("par_in")
        small_in = sem("small_in")
        dtw_in = sem("dtw_in")
        consts_cleared = sem("consts_cleared")
        consts = sem("consts")
        par_t = sem("par_t")
        par_ok = sem("par_ok")
        x_turned = sem("x_turned")
        x_ready = sem("x_ready")
        tile_done = [sem(f"tile_done{s}") for s in range(2)]
        acc_done = sem("acc_done")
        acc_free = [sem(f"acc_free{b}") for b in range(2)]
        silu_done = sem("silu_done")
        h_done = sem("h_done")
        hh_done = sem("hh_done")
        hl_done = sem("hl_done")
        fo_done = sem("fo_done")
        sq_clear = sem("sq_clear")
        sq_added = sem("sq_added")
        out_turned = sem("out_turned")
        out_copied = [sem(f"out_copied{h}") for h in range(2)]
        stored = sem("stored")

        class Norm:

            def __init__(self, n):
                self.sq = sem(f"{n}_sq")
                self.add = sem(f"{n}_add")
                self.sum = sem(f"{n}_sum")
                self.root = sem(f"{n}_root")
                self.rs = sem(f"{n}_rs")
                self.a = sem(f"{n}_a")
                self.val = sem(f"{n}_val")
                self.hi = sem(f"{n}_hi")
                self.lo = sem(f"{n}_lo")

        pre1, post1, prem, postm, pre2, post2 = (Norm(n) for n in ("pre1", "post1", "prem", "postm", "pre2", "post2"))
        ssdn = [Norm(f"ssdn{g}") for g in range(GROUPS)]
        lnn = Norm("lnn")

        dtw_hi = sem("dtw_hi")
        dtw_lo = sem("dtw_lo")
        dt_raw = sem("dt_raw")
        dt_v = sem("dt_v")
        dt_s = sem("dt_s")
        acs_t = sem("acs_t")
        acs_v = sem("acs_v")
        acs_s = sem("acs_s")
        sg_done = sem("sg_done")
        u_done = sem("u_done")
        cv_start = sem("cv_start")
        cv_step = sem("cv_step")
        cv_out = sem("cv_out")
        cb_start = sem("cb_start")
        cb_step = sem("cb_step")
        xbc_done = sem("xbc_done")
        z_done = sem("z_done")
        bt_t = sem("bt_t")
        bt_c = sem("bt_c")
        cbm_t = sem("cbm_t")
        cbm_v = sem("cbm_v")
        xt_t = sem("xt_t")
        xt_v = sem("xt_v")
        xdec_v = sem("xdec_v")
        st_t = sem("st_t")
        st_v = sem("st_v")
        st_m = sem("st_m")
        r_t = sem("r_t")
        seg_s = sem("seg_s")
        le_s = sem("le_s")
        me_v = sem("me_v")
        y_t = sem("y_t")
        y_d = sem("y_d")
        y_v = sem("y_v")
        mu_t = sem("mu_t")
        mu_s = sem("mu_s")
        cen_v = sem("cen_v")
        ln_a = sem("ln_a")
        ln_act = sem("ln_act")

        def wait_tile(eng, b, it, pr):
            if b % 2 == 0:
                eng.wait_ge(tile_done[b // 2], pr + 1)
            else:
                eng.wait_ge(w_used, it * 2 + (1 + b // 2))

        def wait_out(eng, t, it, ac):
            if t == 0:
                eng.wait_ge(acc_done, ac + 1)
            else:
                eng.wait_ge(w_used, it * 2 + 2)

        block = ctx.enter_context(nc.Block())

        @block.sync
        def _(sp):
            for c in range(SC):
                sp.dma_start(x_tok[:, c, :], a["x"][0, c * P:(c + 1) * P, :]).then_inc(x_in[c], 16)

            def load(it, srcs, first=False):
                for s in range(2):
                    if not first:
                        sp.wait_ge(lo_done, it * 2 + (s - 1))
                    kn = srcs[s].shape[1]
                    sp.dma_start(w_raw[s][:, 0:kn * CW].rearrange("p (k n) -> p k n", k=kn),
                                 srcs[s]).then_inc(raw_in[s], 16)

            def ffn(n, it0, first):
                wg, wu, wd = (a[f"ffn{n}_w_{m}"][0].rearrange("(k p) f -> p k f", p=P) for m in ("gate", "up", "down"))
                if first:
                    load(0, [wg[:, :, 0:CW], wu[:, :, 0:CW]], True)
                with sp.Fori(1 if first else 0, FK // 2) as i:
                    load(i + it0, [wg[:, :, bass.ds(i * CW, CW)], wu[:, :, bass.ds(i * CW, CW)]])
                with sp.Fori(0, DK // 2) as m:
                    load(m + (it0 + FK // 2), [wd[:, h * KH:(h + 1) * KH, bass.ds(m * CW, CW)] for h in range(2)])

            ffn(1, IT_GU1, True)
            w_in = a["w_in"][0].rearrange("(k p) f -> p k f", p=P)
            with sp.Fori(0, DK // 2) as i:
                load(i + IT_GLU, [w_in[:, :, bass.ds(i * CW + (GLU0 + j * D_CONV), CW)] for j in range(2)])
            with sp.Fori(0, XT // 4) as i:
                load(i + IT_XBC, [w_in[:, :, bass.ds(i * (2 * CW) + (XBC0 + j * CW), CW)] for j in range(2)])
            with sp.Fori(0, DK // 4) as i:
                load(i + IT_Z, [w_in[:, :, bass.ds(i * (2 * CW) + (Z0 + j * CW), CW)] for j in range(2)])
            w_out = a["w_out"][0].rearrange("(k p) f -> p k f", p=P)
            with sp.Fori(0, DK // 2) as i:
                load(i + IT_OUT, [w_out[:, h * DK:(h + 1) * DK, bass.ds(i * CW, CW)] for h in range(2)])
            ffn(2, IT_GU2, False)
            for c in range(SC):
                for h in range(2):
                    sp.wait_ge(out_copied[h], c + 1)
                sp.dma_start(out[0, c * P:(c + 1) * P, :], x_tok[:, c, :]).then_inc(stored, 16)
            sp.wait_ge(stored, 16 * SC)

        @block.gpsimd
        def _(pool):
            pool.memset(ident[:, :], 0.0).then_inc(consts_cleared, 1)
            pool.memset(tri[:, :], 1.0).then_inc(consts_cleared, 1)
            pool.memset(ones[:, :], 1.0).then_inc(consts, 1)
            pool.memset(eps[:, :], EPS).then_inc(consts, 1)
            pool.wait_ge(consts_cleared, 2)
            pool.affine_select(out=ident[:, :], in_=ident[:, :], compare_op=ALU.not_equal, fill=1.0, base=0,
                               pattern=[[-1, P]], channel_multiplier=1).then_inc(consts, 1)
            pool.affine_select(out=tri[:, :], in_=tri[:, :], compare_op=ALU.is_ge, fill=0.0, base=0,
                               pattern=[[1, P]], channel_multiplier=-1).then_inc(consts, 1)

            def rest(it, kn, first=False):
                for s in range(2):
                    pool.wait_ge(hi_done, it * 2 + (s + 1))
                    if not first:
                        pool.wait_ge(w_used, it * 2 + (s - 1))
                    pool.tensor_tensor(w_lo[s][:, 0:kn * CW], w_raw[s][:, 0:kn * CW], w_hi[s][:, 0:kn * CW].bitcast(F32),
                                       ALU.subtract).then_inc(lo_done, 1)

            rest(0, DK, True)
            with pool.Fori(1, IT_DOWN1) as i:
                rest(i, DK)
            with pool.Fori(IT_DOWN1, IT_GLU) as i:
                rest(i, KH)
            with pool.Fori(IT_GLU, IT_DOWN2) as i:
                rest(i, DK)
            with pool.Fori(IT_DOWN2, IT_END) as i:
                rest(i, KH)

        segments = conv_segments()

        @block.scalar
        def _(act):
            row = 0
            for name, k in VECS:
                act.dma_start(par_rows[row:row + k, 0, :], a[name].rearrange("l (k p) -> (l k) p", p=P)).then_inc(par_in, 16)
                row += k
            act.dma_start(par_rows[0:STAPS * XT, 1, :],
                          a["ssd_conv_w"].rearrange("l j (t p) -> (l j t) p", p=P)).then_inc(par_in, 16)
            cw = a["conf_dw_w"].rearrange("l j (t p) -> (l j t) p", p=P)
            for h in range(2):
                act.dma_start(par_rows[0:HALF_ROWS, 2 + h, :], cw[h * HALF_ROWS:(h + 1) * HALF_ROWS, :]).then_inc(par_in, 16)
            act.dma_start(dtb[:, :], a["dt_bias"].to_broadcast([P, HEADS])).then_inc(small_in, 16)
            act.dma_start(alog[:, :], a["a_log"].to_broadcast([P, HEADS])).then_inc(small_in, 16)
            dsk = a["d_skip"].rearrange("l (t h) -> l h t", h=2)
            with nc.allow_non_contiguous_dma(reason="16 values"):
                for h in range(2):
                    act.dma_start(d_col[h * HD:(h + 1) * HD, :], dsk[:, h, :].to_broadcast([HD, DK])).then_inc(small_in, 16)

            def round_w(it, kn, first=False):
                for s in range(2):
                    act.wait_ge(raw_in[s], it * 16 + 16)
                    if not first:
                        act.wait_ge(w_used, it * 2 + (s - 1))
                    act.activation(w_hi[s][:, 0:kn * CW], w_raw[s][:, 0:kn * CW], ACT.Copy).then_inc(hi_done, 1)

            def square(nm, k, src):
                if k >= 2:
                    act.wait_ge(nm.add, k - 1)
                act.activation(bank[4 + k % 2][:, :], src, ACT.Square).then_inc(nm.sq, 1)

            def root(nm, b, n):
                act.wait_ge(nm.sum, 1)
                act.activation(bank[b][:, :], bank[b][:, :], ACT.Sqrt, bias=eps[:, 0:1], scale=1.0 / n).then_inc(nm.root, 1)

            def round_tiles(nm, dst, src, ks, base=0):
                for k in ks:
                    act.wait_ge(nm.val, k - base + 1)
                    act.activation(dst[:, k, :], src[:, k, :], ACT.Copy).then_inc(nm.hi, 1)

            def pre_norm(nm, ready):
                for k in range(DK):
                    ready(k)
                    square(nm, k, x[:, k, :])
                root(nm, 6, D)
                round_tiles(nm, xh, xv, range(DK))

            def square_y(q):
                g = q // (DK // GROUPS)
                act.wait_ge(y_v, q + 1)
                act.activation(bank[2 + q % 2][:, :], z[:, q, :], ACT.Square).then_inc(ssdn[g].sq, 1)

            def silu_table():
                act.activation(spare[:, 0:1], spare[:, 1:2], ACT.Silu)

            def gate_up(n, it0, pr0):
                def hidden(i):
                    tl = i * 2 + n * FK
                    for t in range(2):
                        wait_tile(act, t, i + it0, i + pr0)
                        act.activation(hs[:, i * 2 + t, :], bank[t][:, :], ACT.Silu).then_inc(silu_done, 1)
                    for t in range(2):
                        act.wait_ge(h_done, tl + (t + 1))
                        act.activation(hh[:, i * 2 + t, :], bank[2 + t][:, :], ACT.Copy).then_inc(hh_done, 1)
                silu_table()
                with act.Fori(0, FK // 2 - 1) as i:
                    round_w(i + (it0 + 1), DK)
                    hidden(i)
                round_w(it0 + FK // 2, KH)
                hidden(FK // 2 - 1)

            def take_out(nm, it0, ac0, kn, kn_next):
                def take(i):
                    for t in range(2):
                        wait_out(act, t, i + it0, i + ac0)
                        act.activation(fo[:, i * 2 + t, :], bank[4 + t][:, :], ACT.Copy).then_inc(fo_done, 1)
                        act.wait_ge(fo_done, i * 2 + (2 * ac0 + t + 1))
                        act.activation(bank[4 + t][:, :], bank[4 + t][:, :], ACT.Square).then_inc(nm.sq, 1)
                with act.Fori(0, DK // 2 - 1) as i:
                    round_w(i + (it0 + 1), kn)
                    take(i)
                if kn_next:
                    round_w(it0 + DK // 2, kn_next)
                take(DK // 2 - 1)
                root(nm, 6, D)

            round_w(0, DK, True)
            for k in range(DK):
                act.wait_ge(x_turned, k + 1)
                act.activation(x[:, k, :], bank[k][:, :], ACT.Copy).then_inc(x_ready, 1)
            pre_norm(pre1, lambda k: act.wait_ge(x_ready, DK))
            gate_up(0, IT_GU1, PR_GU1)
            take_out(post1, IT_DOWN1, AC_DOWN1, KH, DK)
            act.wait_ge(w_used, 2 * IT_GLU)
            act.dma_start(dtw[:, :, :], a["w_in"][0].rearrange("(k p) f -> p k f", p=P)[:, :, DT0:DT0 + HEADS]).then_inc(dtw_in, 16)
            pre_norm(prem, lambda k: act.wait_ge(post1.val, k + 1))
            act.wait_ge(dtw_in, 16)
            act.activation(dtwh[:, :, :], dtw[:, :, :], ACT.Copy).then_inc(dtw_hi, 1)

            def conv_open(q):
                for e in range(2):
                    c = 2 * q + e
                    act.wait_ge(u_done, c + 1)
                    if q:
                        act.wait_ge(cv_out, c - 1)
                    act.activation(bank[4 + e][:, :], u[:, c, :], ACT.Identity, bias=col("conf_dw_b", c),
                                   scale=col("conf_dw_w", (TAPS - 1) * DK + c)).then_inc(cv_start, 1)

            def conv_close(q):
                for e in range(2):
                    act.wait_ge(cv_step, (q + 1) * 2 * (TAPS - 1) - 1 + e)
                    act.activation(u[:, 2 * q + e, :], bank[4 + e][:, :], ACT.Copy).then_inc(cv_out, 1)

            def conv_turns(n):
                for q, s in segments[n]:
                    if s == 1:
                        conv_open(q)
                    if s == TAPS - 1:
                        conv_close(q)

            for i in range(DK // 2):
                round_w(IT_GLU + i + 1, DK)
                for t in range(2):
                    c = 2 * i + t
                    wait_tile(act, 2 + t, IT_GLU + i, PR_GLU + i)
                    if c >= 2:
                        act.wait_ge(u_done, c - 1)
                    act.activation(sg[:, t, :], bank[2 + t][:, :], ACT.Sigmoid, bias=col("b_glu", DK + c)).then_inc(sg_done, 1)
                conv_turns(i)
            act.wait_ge(dt_v, 1)
            act.activation(t_abs[:, :, :], dt_tok[:, :, :], ACT.Abs).then_inc(dt_s, 1)
            act.wait_ge(dt_s, 1)
            act.activation(t_abs[:, :, :], t_abs[:, :, :], ACT.Exp, scale=-1.0).then_inc(dt_s, 1)
            act.wait_ge(dt_s, 2)
            act.activation(t_abs[:, :, :], t_abs[:, :, :], ACT.Ln, bias=1.0).then_inc(dt_s, 1)
            act.wait_ge(small_in, 64)
            act.activation(alog[:, :], alog[:, :], ACT.Exp).then_inc(dt_s, 1)
            act.wait_ge(acs_v, 2)
            act.activation(wdec[:, :, :], wdec[:, :, :], ACT.Exp).then_inc(acs_s, 1)
            act.activation(dend[:, :, :].rearrange("p c h -> p (c h)"), bank[7][:, 64:128], ACT.Exp).then_inc(acs_s, 1)
            for i in range(XT // 4):
                round_w(IT_XBC + i + 1, DK)
                for b in range(4):
                    c = 4 * i + b
                    wait_tile(act, b, IT_XBC + i, PR_XBC + i)
                    act.activation(xbc[:, c, :], bank[b][:, :], ACT.Identity, bias=col("ssd_conv_b", c),
                                   scale=col("ssd_conv_w", (STAPS - 1) * XT + c)).then_inc(cb_start, 1)
                for b in range(4):
                    c = 4 * i + b
                    act.wait_ge(cb_step, short_steps(c))
                    act.activation(xbc[:, c, :], xbc[:, c, :], ACT.Silu).then_inc(xbc_done, 1)
                conv_turns(DK // 2 + i)
            for i in range(DK // 4):
                round_w(IT_Z + i + 1, DK)
                for b in range(4):
                    wait_tile(act, b, IT_Z + i, PR_Z + i)
                    act.activation(z[:, 4 * i + b, :], bank[b][:, :], ACT.Silu).then_inc(z_done, 1)
                conv_turns(DK // 2 + XT // 4 + i)
            for g in range(GROUPS):
                act.wait_ge(bt_t, g + 1)
                act.activation(b_tok[:, g, :, :].rearrange("p c n -> p (c n)"), bank[6 + g][:, :], ACT.Copy).then_inc(bt_c, 1)
            for h in range(HEADS):
                act.wait_ge(r_t, h + 1)
                if h >= 2:
                    act.wait_ge(me_v, 2 * (h - 1))
                for c in range(SC):
                    act.activation(l_t[:, h % 2, c * P:(c + 1) * P], bank[h % 2][:, c * P:(c + 1) * P], ACT.Relu,
                                   bias=acs[:, c, h:h + 1], scale=-1.0).then_inc(seg_s, 1)
                if h >= 2:
                    act.wait_ge(y_t, h - 1)
                act.activation(e_t[:, h % 2, :], bank[h % 2][:, :], ACT.Exp).then_inc(le_s, 1)
                act.wait_ge(seg_s, SC * (h + 1))
                act.activation(l_t[:, h % 2, :], l_t[:, h % 2, :], ACT.Exp, scale=-1.0).then_inc(le_s, 1)
                if h % 2:
                    q = h // 2
                    if q:
                        square_y(q - 1)
            square_y(DK - 1)
            conv_turns(len(CONV_PLAN) - 1)
            for g in range(GROUPS):
                root(ssdn[g], 6 + g, D_SSM // GROUPS)
            for g in range(GROUPS):
                round_tiles(ssdn[g], ysh, z, range(4 * g, 4 * g + 4), 4 * g)
            act.wait_ge(mu_t, 1)
            act.activation(bank[4][:, :], bank[4][:, :], ACT.Copy, scale=-1.0 / D_CONV).then_inc(mu_s, 1)
            for c in range(DK):
                act.wait_ge(cen_v, c + 1)
                if c >= 2:
                    act.wait_ge(lnn.add, c - 1)
                act.activation(bank[c % 2][:, :], u[:, c, :], ACT.Square).then_inc(lnn.sq, 1)
            root(lnn, 5, D_CONV)
            silu_table()
            for c in range(DK):
                act.wait_ge(lnn.val, c + 1)
                act.activation(u[:, c, :], u[:, c, :], ACT.Silu, bias=col("conf_ln_b", c)).then_inc(ln_act, 1)
                act.wait_ge(ln_act, c + 1)
                act.activation(ych[:, c, :], u[:, c, :], ACT.Copy).then_inc(lnn.hi, 1)

            take_out(postm, IT_OUT, AC_OUT, DK, DK)
            pre_norm(pre2, lambda k: act.wait_ge(postm.val, k + 1))
            gate_up(1, IT_GU2, PR_GU2)
            take_out(post2, IT_DOWN2, AC_DOWN2, KH, 0)
            for c in range(SC):
                act.wait_ge(out_turned, 2 * c + 1)
                act.activation(x_tok[:, c, 0:T], bank[2 * c][:, :], ACT.Copy).then_inc(out_copied[0], 1)

        @block.vector
        def _(dve):
            def add_square(nm, k, b, total):
                dve.wait_ge(nm.sq, k + 1)
                if k == 0:
                    dve.tensor_copy(total, bank[b][:, :]).then_inc(nm.add, 1)
                else:
                    dve.wait_ge(nm.add, k)
                    dve.tensor_tensor(total, total, bank[b][:, :], ALU.add).then_inc(nm.add, 1)

            def invert(nm, b):
                dve.wait_ge(nm.root, 1)
                dve.reciprocal(bank[b][:, :], bank[b][:, :]).then_inc(nm.rs, 1)
                dve.wait_ge(nm.rs, 1)

            def split(nm, val, hi, lo, gain, b, ks, src=None):
                ks = list(ks)

                def rest(k):
                    dve.wait_ge(nm.hi, k - ks[0] + 1)
                    dve.tensor_tensor(lo[:, k, :], val[:, k, :], hi[:, k, :].bitcast(F32), ALU.subtract).then_inc(nm.lo, 1)
                for k in ks:
                    dve.scalar_tensor_tensor(out=val[:, k, :], in0=(src or val)[:, k, :], scalar=col(gain, k),
                                             in1=bank[b][:, :], op0=ALU.mult, op1=ALU.mult).then_inc(nm.val, 1)
                    if k > ks[0]:
                        rest(k - 1)
                rest(ks[-1])

            def pre_norm(nm, gain):
                for k in range(DK):
                    add_square(nm, k, 4 + k % 2, sq_norm[:, :])
                invert(nm, 6)
                split(nm, xv, xh, xl, gain, 6, range(DK), x)

            def gate_up(n, it0, pr0):
                with dve.Fori(0, FK // 2) as i:
                    tl = i * 2 + n * FK
                    for t in range(2):
                        dve.wait_ge(silu_done, tl + (t + 1))
                        wait_tile(dve, 2 + t, i + it0, i + pr0)
                        dve.tensor_tensor(bank[2 + t][:, :], hs[:, i * 2 + t, :], bank[2 + t][:, :], ALU.mult).then_inc(h_done, 1)
                    for t in range(2):
                        dve.wait_ge(hh_done, tl + (t + 1))
                        dve.tensor_tensor(hl[:, i * 2 + t, :], bank[2 + t][:, :], hh[:, i * 2 + t, :].bitcast(F32),
                                          ALU.subtract).then_inc(hl_done, 1)

            def post_norm(nm, n, ac0, gain, ready):
                ready()
                dve.memset(sq_norm[:, :], 0.0).then_inc(sq_clear, 1)
                dve.wait_ge(sq_clear, n + 1)
                with dve.Fori(0, DK // 2) as i:
                    for t in range(2):
                        dve.wait_ge(nm.sq, i * 2 + (t + 1))
                        if t:
                            dve.wait_ge(acc_free[0], i + (ac0 + 1))
                        elif ac0:
                            dve.wait_ge(acc_free[1], i + ac0)
                        else:
                            dve.wait_ge(sq_clear, i * 0 + 1)
                        dve.tensor_tensor(sq_norm[:, :], sq_norm[:, :], bank[4 + t][:, :], ALU.add).then_inc(acc_free[t], 1)
                invert(nm, 6)
                for k in range(DK):
                    dve.tensor_tensor(fo[:, k, :], fo[:, k, :], bank[6][:, :], ALU.mult).then_inc(nm.a, 1)
                    if k:
                        step(nm, k - 1, gain)
                step(nm, DK - 1, gain)

            def step(nm, k, gain):
                dve.wait_ge(nm.a, k + 1)
                dve.scalar_tensor_tensor(out=x[:, k, :], in0=fo[:, k, :], scalar=col(gain, k), in1=x[:, k, :],
                                         op0=ALU.mult, op1=ALU.add).then_inc(nm.val, 1)

            dve.memset(spare[:, :], 0.0).then_inc(par_ok, 1)
            dve.wait_ge(par_t, 1)
            dve.tensor_copy(par[:, :], bank[7][:, 0:NPAR]).then_inc(par_ok, 1)
            dve.wait_ge(par_ok, 2)
            for name in ("ffn1_post_g", "ffn2_post_g"):
                g = par[:, COL[name]:COL[name] + DK]
                dve.tensor_scalar(g, g, 0.5, None, ALU.mult).then_inc(par_ok, 1)
            dve.wait_ge(par_ok, 4)

            pre_norm(pre1, "ffn1_pre_g")
            gate_up(0, IT_GU1, PR_GU1)
            post_norm(post1, 0, AC_DOWN1, "ffn1_post_g", lambda: dve.wait_ge(w_used, 2 * IT_DOWN1))
            pre_norm(prem, "mix_pre_g")
            dve.wait_ge(dtw_hi, 1)
            dve.tensor_tensor(dtwl[:, :, :], dtw[:, :, :], dtwh[:, :, :].bitcast(F32), ALU.subtract).then_inc(dtw_lo, 1)

            def conv(n):
                for q, s in segments[n]:
                    for e in range(2):
                        c, done = 2 * q + e, 2 * (q * (TAPS - 1) + s - 1) + e
                        if s == 1:
                            dve.wait_ge(cv_start, c + 1)
                        else:
                            dve.wait_ge(cv_step, done - 1)
                        dve.scalar_tensor_tensor(out=bank[4 + e][:, s:], in0=u[:, c, 0:T - s],
                                                 scalar=col("conf_dw_w", (TAPS - 1 - s) * DK + c),
                                                 in1=bank[4 + e][:, s:], op0=ALU.mult, op1=ALU.add).then_inc(cv_step, 1)

            for i in range(DK // 2):
                for t in range(2):
                    c = 2 * i + t
                    wait_tile(dve, t, IT_GLU + i, PR_GLU + i)
                    dve.wait_ge(sg_done, c + 1)
                    dve.scalar_tensor_tensor(out=u[:, c, :], in0=bank[t][:, :], scalar=col("b_glu", c), in1=sg[:, t, :],
                                             op0=ALU.add, op1=ALU.mult).then_inc(u_done, 1)
                if i == 0:
                    dve.wait_ge(dt_raw, 1)
                    dve.wait_ge(small_in, 64)
                    dve.tensor_tensor(dt_tok[:, :, :], bank[7][:, 0:SC * HEADS].rearrange("p (c h) -> p c h", c=SC),
                                      dtb[:, :].unsqueeze(1).to_broadcast([P, SC, HEADS]), ALU.add).then_inc(dt_v, 1)
                conv(i)
            dve.wait_ge(dt_s, 4)
            dve.scalar_tensor_tensor(out=dt_tok[:, :, :], in0=dt_tok[:, :, :], scalar=0.0, in1=t_abs[:, :, :],
                                     op0=ALU.max, op1=ALU.add).then_inc(dt_v, 1)
            dve.wait_ge(dt_v, 2)
            dve.scalar_tensor_tensor(out=da_tok[:, :, :], in0=dt_tok[:, :, :], scalar=-1.0,
                                     in1=alog[:, :].unsqueeze(1).to_broadcast([P, SC, HEADS]),
                                     op0=ALU.mult, op1=ALU.mult).then_inc(dt_v, 1)
            dve.wait_ge(acs_t, 1)
            dve.tensor_copy(acs[:, :, :].rearrange("p c h -> p (c h)"), bank[7][:, 0:64]).then_inc(acs_v, 1)
            dve.wait_ge(acs_v, 1)
            dve.tensor_tensor(wdec[:, :, :].rearrange("p c h -> p (c h)"), bank[7][:, 64:128],
                              acs[:, :, :].rearrange("p c h -> p (c h)"), ALU.subtract).then_inc(acs_v, 1)
            dve.wait_ge(acs_s, 2)
            dve.tensor_tensor(wdec[:, :, :], wdec[:, :, :], dt_tok[:, :, :], ALU.mult).then_inc(acs_v, 1)
            for i in range(XT // 4):
                for b0 in (0, 2):
                    for s in range(1, STAPS):
                        for e in range(2):
                            b = b0 + e
                            c = 4 * i + b
                            done = short_steps(c) - 1 - 2 * (STAPS - 1 - s)
                            if s == 1:
                                dve.wait_ge(cb_start, c + 1)
                            else:
                                dve.wait_ge(cb_step, done - 1)
                            dve.scalar_tensor_tensor(out=xbc[:, c, s:], in0=bank[b][:, 0:T - s],
                                                     scalar=col("ssd_conv_w", (STAPS - 1 - s) * XT + c),
                                                     in1=xbc[:, c, s:], op0=ALU.mult, op1=ALU.add).then_inc(cb_step, 1)
                conv(DK // 2 + i)
            for i in range(DK // 4):
                conv(DK // 2 + XT // 4 + i)
            for g in range(GROUPS):
                dve.wait_ge(cbm_t, g + 1)
                dve.tensor_tensor(g_mask[:, g, :, :], bank[g][:, :].rearrange("p (c t) -> p c t", c=SC),
                                  tri[:, :].unsqueeze(1).to_broadcast([P, SC, P]), ALU.mult).then_inc(cbm_v, 1)
            dve.wait_ge(acs_v, 3)

            def state(n):
                c, g = n // 2, n % 2
                gs = slice(g * T, (g + 1) * T)
                dve.wait_ge(st_t, n + 1)
                if c == 0:
                    dve.tensor_copy(hst[:, 0, gs], bank[g][:, :]).then_inc(st_v, 1)
                    return
                dve.wait_ge(st_v, n - 1)
                dve.tensor_tensor(hst[:, c, gs].rearrange("p (h d) -> p h d", d=HD),
                                  hst[:, c - 1, gs].rearrange("p (h d) -> p h d", d=HD),
                                  dend[:, c, g * HG:(g + 1) * HG].unsqueeze(2).to_broadcast([P, HG, HD]),
                                  ALU.mult).then_inc(st_m, 1)
                dve.wait_ge(st_m, n - 1)
                dve.tensor_tensor(hst[:, c, gs], hst[:, c, gs], bank[g][:, :], ALU.add).then_inc(st_v, 1)

            for n in range(2 * SC):
                c, g = n // 2, n % 2
                dve.wait_ge(xt_t, n + 1)
                src = bank[2 + g][:, :].rearrange("p (h d) -> p h d", d=HD)
                hg = slice(g * HG, (g + 1) * HG)
                if c < SC - 1:
                    if n >= 2:
                        dve.wait_ge(st_t, n - 1)
                    dve.tensor_tensor(x_dec[:, g, :].rearrange("p (h d) -> p h d", d=HD), src,
                                      wdec[:, c, hg].unsqueeze(2).to_broadcast([P, HG, HD]), ALU.mult).then_inc(xdec_v, 1)
                dve.tensor_tensor(x_dt[:, c, g * T:(g + 1) * T].rearrange("p (h d) -> p h d", d=HD), src,
                                  dt_tok[:, c, hg].unsqueeze(2).to_broadcast([P, HG, HD]), ALU.mult).then_inc(xt_v, 1)
                if 1 <= n <= 2 * SC - 2:
                    state(n - 1)

            def gated(q):
                g, b = q // (DK // GROUPS), 2 + q % 2
                dve.wait_ge(y_t, 2 * q + 2)
                dve.scalar_tensor_tensor(out=bank[b][:, :], in0=xbc[:, q, :], scalar=d_col[:, q:q + 1],
                                         in1=bank[b][:, :], op0=ALU.mult, op1=ALU.add).then_inc(y_d, 1)
                dve.wait_ge(y_d, q + 1)
                dve.tensor_tensor(z[:, q, :], z[:, q, :], bank[b][:, :], ALU.mult).then_inc(y_v, 1)

            def add_y(q):
                g = q // (DK // GROUPS)
                add_square(ssdn[g], q % (DK // GROUPS), 2 + q % 2, sq_ssd[:, g, :])

            dve.wait_ge(z_done, DK)
            for h in range(HEADS):
                g = h // HG
                dve.wait_ge(le_s, 2 * h + 2)
                if h >= 2:
                    dve.wait_ge(y_t, h - 1)
                dve.tensor_tensor(m_t[:, h % 2, :], l_t[:, h % 2, :], g_mask[:, g, :, :].rearrange("p c t -> p (c t)"),
                                  ALU.mult).then_inc(me_v, 1)
                dve.tensor_tensor(e_t[:, h % 2, P:], e_t[:, h % 2, P:], xbc[:, D_SSM // P + GROUPS + g, P:],
                                  ALU.mult).then_inc(me_v, 1)
                if h % 2 and h > 1:
                    gated(h // 2 - 1)
                if h % 2 == 0 and h > 2:
                    add_y(h // 2 - 2)
            add_y(DK - 2)
            gated(DK - 1)
            add_y(DK - 1)
            conv(len(CONV_PLAN) - 1)
            for g in range(GROUPS):
                invert(ssdn[g], 6 + g)
            for g in range(GROUPS):
                split(ssdn[g], z, ysh, ysl, "ssd_norm_g", 6 + g, range(4 * g, 4 * g + 4))
            dve.wait_ge(mu_s, 1)
            for c in range(DK):
                dve.tensor_tensor(u[:, c, :], u[:, c, :], bank[4][:, :], ALU.add).then_inc(cen_v, 1)
                if c:
                    add_square(lnn, c - 1, (c - 1) % 2, sq_ln[:, :])
            add_square(lnn, DK - 1, (DK - 1) % 2, sq_ln[:, :])
            invert(lnn, 5)
            for c in range(DK):
                dve.scalar_tensor_tensor(out=u[:, c, :], in0=u[:, c, :], scalar=col("conf_ln_g", c), in1=bank[5][:, :],
                                         op0=ALU.mult, op1=ALU.mult).then_inc(lnn.val, 1)
            for c in range(DK):
                dve.wait_ge(lnn.hi, c + 1)
                dve.tensor_tensor(ycl[:, c, :], u[:, c, :], ych[:, c, :].bitcast(F32), ALU.subtract).then_inc(lnn.lo, 1)

            post_norm(postm, 1, AC_OUT, "mix_post_g", lambda: dve.wait_ge(y_t, HEADS))
            pre_norm(pre2, "ffn2_pre_g")
            gate_up(1, IT_GU2, PR_GU2)
            post_norm(post2, 2, AC_DOWN2, "ffn2_post_g", lambda: dve.wait_ge(w_used, 2 * IT_DOWN2))
            for c in range(SC):
                dve.wait_ge(out_turned, 2 * c + 2)
                dve.tensor_copy(x_tok[:, c, T:2 * T], bank[2 * c + 1][:, :]).then_inc(out_copied[1], 1)

        @block.tensor
        def _(pe):
            def three(dst, s, blk, t, hi, lo, first, last):
                c0 = blk * CW + t * P
                pe.matmul(dst, w_lo[s][:, c0:c0 + P], hi, start=first, stop=False)
                pe.matmul(dst, w_hi[s][:, c0:c0 + P], lo, start=False, stop=False)
                return pe.matmul(dst, w_hi[s][:, c0:c0 + P], hi, start=False, stop=last)

            def project(it, free):
                for s in range(2):
                    pe.wait_ge(lo_done, it * 2 + (s + 1))
                    for t in range(2):
                        for sm, v in free(2 * s + t):
                            pe.wait_ge(sm, v)
                        for k in range(DK):
                            last = three(bank[2 * s + t][:, :], s, k, t, xh[:, k, :], xl[:, k, :], k == 0, k == DK - 1)
                        last.then_inc(w_used if t else tile_done[s], 1)

            def turned_sum(nm, total, b):
                pe.matmul(bank[b][:, :], ones[:, :], total, start=True, stop=True).then_inc(nm.sum, 1)

            def gate_up(n, it0, prev):
                def free(i):
                    tl = i * 2 + (n * FK - 1)
                    return lambda b: [(silu_done if b < 2 else hl_done, tl + b % 2)]
                project(it0, prev)
                with pe.Fori(1, FK // 2) as i:
                    project(i + it0, free(i))

            def reduce_out(it0, ac0, halves, kn, ready):
                def pair(i, first):
                    for s in range(2):
                        pe.wait_ge(lo_done, i * 2 + (2 * it0 + s + 1))
                        for t in range(2):
                            if s == 0 and not first:
                                pe.wait_ge(acc_free[t], i + ac0)
                            for k in range(kn):
                                hi, lo = halves(s * kn + k)
                                last = three(bank[4 + t][:, :], s, k, t, hi, lo, s + k == 0, s == 1 and k == kn - 1)
                            if t:
                                last.then_inc(w_used, 1)
                            elif s:
                                last.then_inc(acc_done, 1)
                ready()
                pair(0, ac0 == 0)
                with pe.Fori(1, DK // 2) as i:
                    pair(i, False)

            def pre_norm(nm):
                pe.wait_ge(nm.add, DK)
                turned_sum(nm, sq_norm[:, :], 6)

            def post_norm(nm, ac0):
                for t in range(2):
                    pe.wait_ge(acc_free[t], ac0 + DK // 2)
                turned_sum(nm, sq_norm[:, :], 6)

            def hidden(n):
                def ready():
                    pe.wait_ge(hh_done, (n + 1) * FK)
                    pe.wait_ge(hl_done, (n + 1) * FK)
                return ready

            pe.wait_ge(consts, 4)
            pe.wait_ge(par_in, 16 * (len(VECS) + 3))
            at_col = 0
            for i, rows in enumerate((NVEC, STAPS * XT, HALF_ROWS, HALF_ROWS)):
                last = pe.transpose(bank[7][:, at_col:at_col + rows], par_rows[0:rows, i, :], ident[0:rows, 0:rows])
                at_col += rows
            last.then_inc(par_t, 1)
            for c in range(SC):
                pe.wait_ge(x_in[c], 16)
            for k in range(DK):
                if k == 7:
                    pe.wait_ge(par_ok, 2)
                for c in range(SC):
                    last = pe.transpose(bank[k][:, c * P:(c + 1) * P], x_tok[:, c, k * P:(k + 1) * P], ident[:, :])
                last.then_inc(x_turned, 1)
            pre_norm(pre1)
            pe.wait_ge(pre1.lo, DK)
            gate_up(0, IT_GU1, lambda b: [])
            reduce_out(IT_DOWN1, AC_DOWN1, lambda k: (hh[:, k, :], hl[:, k, :]), KH, hidden(0))
            post_norm(post1, AC_DOWN1)
            pre_norm(prem)
            pe.wait_ge(prem.lo, DK)

            pe.wait_ge(dtw_lo, 1)
            for c in range(SC):
                cs = slice(c * P, (c + 1) * P)
                for k in range(DK):
                    dst = bank[7][:, c * HEADS:(c + 1) * HEADS]
                    pe.matmul(dst, xl[:, k, cs], dtwh[:, k, :], start=(k == 0), stop=False)
                    pe.matmul(dst, xh[:, k, cs], dtwl[:, k, :], start=False, stop=False)
                    last = pe.matmul(dst, xh[:, k, cs], dtwh[:, k, :], start=False, stop=(k == DK - 1))
            last.then_inc(dt_raw, 1)
            for i in range(DK // 2):
                project(IT_GLU + i, lambda b: [(silu_done if b < 2 else hl_done, FK)] if i == 0 else
                        [(u_done if b < 2 else sg_done, 2 * i - 1 + b % 2)])
            pe.wait_ge(dt_v, 3)
            da = da_tok[:, :, :].rearrange("p c h -> p (c h)")
            pe.matmul(bank[7][:, 0:64], tri[:, :], da, start=True, stop=True)
            pe.matmul(bank[7][:, 64:128], ones[:, :], da, start=True, stop=True).then_inc(acs_t, 1)
            for i in range(XT // 4):
                project(IT_XBC + i, lambda b: [(u_done if b < 2 else sg_done, DK - 1 + b % 2)] if i == 0 else
                        [(cb_step, short_steps(4 * (i - 1) + b))])
            for i in range(DK // 4):
                project(IT_Z + i, lambda b: [(cb_step, short_steps(XT - 4 + b)), (xbc_done, XT)] if i == 0 else
                        [(z_done, 4 * (i - 1) + b + 1)])

            pe.wait_ge(acs_s, 2)
            pe.wait_ge(xbc_done, XT)
            for g in range(GROUPS):
                for c in range(SC):
                    last = pe.transpose(bank[6 + g][:, c * P:(c + 1) * P], xbc[:, DK + g, c * P:(c + 1) * P], ident[:, :])
                last.then_inc(bt_t, 1)
            pe.wait_ge(z_done, DK)
            for g in range(GROUPS):
                for c in range(SC):
                    cs = slice(c * P, (c + 1) * P)
                    last = pe.matmul(bank[g][:, cs], xbc[:, DK + g, cs], xbc[:, DK + GROUPS + g, cs], start=True, stop=True)
                last.then_inc(cbm_t, 1)

            def turn_x(n):
                c, g = n // 2, n % 2
                if n >= 2:
                    pe.wait_ge(xt_v, n - 1)
                for j in range(4):
                    last = pe.transpose(bank[2 + g][:, j * P:(j + 1) * P], xbc[:, 4 * g + j, c * P:(c + 1) * P], ident[:, :])
                last.then_inc(xt_t, 1)

            def state(n):
                c, g = n // 2, n % 2
                pe.wait_ge(xdec_v, n + 1)
                if n >= 2:
                    pe.wait_ge(st_v, n - 1)
                else:
                    pe.wait_ge(cbm_v, n + 1)
                pe.matmul(bank[g][:, :], b_tok[:, g, c, :], x_dec[:, g, :], start=True, stop=True).then_inc(st_t, 1)

            turn_x(0)
            turn_x(1)
            pe.wait_ge(bt_c, 2)
            for n in range(2 * SC):
                if n < 2 * SC - 2:
                    state(n)
                    turn_x(n + 2)

            def decays(h):
                if h >= 2:
                    pe.wait_ge(le_s, 2 * (h - 1))
                else:
                    pe.wait_ge(st_v, 2 * SC - 2)
                for c in range(SC):
                    last = pe.matmul(bank[h % 2][:, c * P:(c + 1) * P], da_tok[:, c, h:h + 1].to_broadcast([P, P]),
                                     tri[:, :], start=True, stop=True)
                last.then_inc(r_t, 1)

            def scan(h):
                q, half = h // 2, h % 2
                pe.wait_ge(me_v, 2 * h + 2)
                if half == 0:
                    if q < 2:
                        pe.wait_ge(xt_v, 2 * SC)
                    else:
                        qq = q - 2
                        pe.wait_ge(ssdn[qq // 4].add, qq % 4 + 1)
                for c in range(SC):
                    cs = slice(c * P, (c + 1) * P)
                    dst = bank[2 + q % 2][half * HD:(half + 1) * HD, cs]
                    hd = slice(h * HD, (h + 1) * HD)
                    last = pe.matmul(dst, x_dt[:, c, hd], m_t[:, half, cs], start=True, stop=(c == 0))
                    if c:
                        last = pe.matmul(dst, hst[:, c - 1, hd], e_t[:, half, cs], start=False, stop=True)
                last.then_inc(y_t, 1)

            decays(0)
            decays(1)
            for h in range(HEADS):
                if h + 2 < HEADS:
                    decays(h + 2)
                scan(h)
            for g in range(GROUPS):
                pe.wait_ge(ssdn[g].add, DK // GROUPS)
                turned_sum(ssdn[g], sq_ssd[:, g, :], 6 + g)
            for c in range(DK):
                pe.wait_ge(cv_out, c + 1 if c else 2 * CONV_PAIRS)
                last = pe.matmul(bank[4][:, :], ones[:, :], u[:, c, :], start=(c == 0), stop=(c == DK - 1))
            last.then_inc(mu_t, 1)
            pe.wait_ge(lnn.add, DK)
            turned_sum(lnn, sq_ln[:, :], 5)

            def mixed():
                for nm, n in ((ssdn[0], 4), (ssdn[1], 4), (lnn, DK)):
                    pe.wait_ge(nm.lo, n)
            reduce_out(IT_OUT, AC_OUT, lambda k: (ysh[:, k, :], ysl[:, k, :]) if k < DK else
                       (ych[:, k - DK, :], ycl[:, k - DK, :]), DK, mixed)
            post_norm(postm, AC_OUT)
            pre_norm(pre2)
            pe.wait_ge(pre2.lo, DK)
            gate_up(1, IT_GU2, lambda b: [])
            reduce_out(IT_DOWN2, AC_DOWN2, lambda k: (hh[:, k, :], hl[:, k, :]), KH, hidden(1))
            post_norm(post2, AC_DOWN2)
            pe.wait_ge(post2.val, DK)
            for c in range(SC):
                for h in range(2):
                    for j in range(4):
                        last = pe.transpose(bank[2 * c + h][:, j * P:(j + 1) * P], x[:, 4 * h + j, c * P:(c + 1) * P], ident[:, :])
                    last.then_inc(out_turned, 1)


def short_steps(c):
    return (c // 2) * 2 * (STAPS - 1) + 2 * (STAPS - 2) + c % 2 + 1


_INS = ["x", "ffn1_pre_g", "ffn1_w_gate", "ffn1_w_up", "ffn1_w_down", "ffn1_post_g", "mix_pre_g", "w_in", "b_glu",
        "ssd_conv_w", "ssd_conv_b", "dt_bias", "a_log", "d_skip", "ssd_norm_g", "conf_dw_w", "conf_dw_b",
        "conf_ln_g", "conf_ln_b", "w_out", "mix_post_g", "ffn2_pre_g", "ffn2_w_gate", "ffn2_w_up", "ffn2_w_down",
        "ffn2_post_g"]


def kernel(**inputs):
    import numpy as _np
    import concourse.bacc as _bacc
    from concourse import mybir as _mybir
    from concourse.bass_utils import run_bass_kernel_spmd as _run

    nc = _bacc.Bacc("TRN2", target_bir_lowering=False, num_devices=1)
    arrays, args = {}, {}
    for name in _INS:
        arr = _np.ascontiguousarray(inputs[name])
        arrays[f"in_{name}"] = arr
        args[name] = nc.dram_tensor(f"in_{name}", arr.shape, _mybir.dt.from_np(arr.dtype), kind="ExternalInput").ap()
    out = nc.dram_tensor("out_x", (1, T, D), F32, kind="ExternalOutput").ap()
    build(nc, args, out)
    r = _run(nc, [arrays], core_ids=[0])
    return r.results[0]["out_x"]
```

```python
from contextlib import ExitStack

import concourse.bass as bass
from concourse import mybir

ALU = mybir.AluOpType
ACT = mybir.ActivationFunctionType
F32 = mybir.dt.float32
F32R = mybir.dt.float32r

P = 128
T = 512
D = 1024
FF = 2816
DK = D // P
FK = FF // P
KH = FK // 2
CW = 256
D_SSM = 1024
STATE = 128
GROUPS = 2
HEADS = 16
HD = 64
XBC = D_SSM + 2 * GROUPS * STATE
XT = XBC // P
D_CONV = 1024
TAPS = 31
STAPS = 4
SC = T // P
HG = HEADS // GROUPS
EPS = 1e-6

Z0 = 0
XBC0 = D_SSM
DT0 = XBC0 + XBC
GLU0 = DT0 + HEADS

IT_GU1 = 0
IT_DOWN1 = IT_GU1 + FK // 2
IT_GLU = IT_DOWN1 + DK // 2
IT_XBC = IT_GLU + DK // 2
IT_Z = IT_XBC + XT // 4
IT_OUT = IT_Z + DK // 4
IT_GU2 = IT_OUT + DK // 2
IT_DOWN2 = IT_GU2 + FK // 2
IT_END = IT_DOWN2 + DK // 2
PR_GU1 = 0
PR_GLU = FK // 2
PR_XBC = PR_GLU + DK // 2
PR_Z = PR_XBC + XT // 4
PR_GU2 = PR_Z + DK // 4
AC_DOWN1 = 0
AC_OUT = DK // 2
AC_DOWN2 = DK

VECS = [("ffn1_pre_g", 8), ("ffn1_post_g", 8), ("mix_pre_g", 8), ("mix_post_g", 8), ("ffn2_pre_g", 8),
        ("ffn2_post_g", 8), ("ssd_norm_g", 8), ("conf_ln_g", 8), ("conf_ln_b", 8), ("conf_dw_b", 8),
        ("b_glu", 16), ("ssd_conv_b", 12)]
COL = {}
_at = 0
for _n, _k in VECS:
    COL[_n] = _at
    _at += _k
NVEC = _at
COL["ssd_conv_w"] = NVEC
COL["conf_dw_w"] = NVEC + STAPS * XT
HALF_ROWS = TAPS * DK // 2
NPAR = NVEC + STAPS * XT + TAPS * DK


STEPS = TAPS - 1
DVE_STEPS = [0, 0, 12, 12, 8, 8, 8, 12, 0, 0]
POOL_STEPS = [0, 5, 5, 5, 5, 5, 5, 5, 5, 20]
POOL_PAIRS = 2


def starts(plan):
    return [sum(plan[:n]) for n in range(len(plan) + 1)]


DVE_AT, POOL_AT = starts(DVE_STEPS), starts(POOL_STEPS)
assert DVE_AT[-1] == POOL_AT[-1] == POOL_PAIRS * STEPS

OUT_CHUNKS = [(0, 0), (0, 1), (0, 2), (1, 0), (1, 1), (1, 2), (0, 3), (1, 3)]


def out_bank(m):
    return m if m < 6 else m - 6


def turn_bank(k):
    return 4 + k % 3


def build(nc, a, out):
    ctx = ExitStack()
    with ctx:
        def sem(name):
            return ctx.enter_context(nc.semaphore(name))

        top = [(nc.sbuf_base + 63) // 64 * 64]

        def region(size):
            at = top[0]
            top[0] += (size + 31) // 32 * 32
            assert top[0] <= nc.sbuf_usable_end, (top[0], nc.sbuf_usable_end)
            return at

        def at(name, shape, dt, offset):
            return nc.alloc_sbuf_tensor_at(name, shape, dt, offset=offset)

        WB = KH * CW * 4
        TB = T * 4
        raw_at = [region(WB) for _ in range(2)]
        w_raw = [at(f"w_raw{s}", [P, KH * CW], F32, raw_at[s]) for s in range(2)]
        hi_at = [region(WB) for _ in range(2)]
        lo_at = [region(WB) for _ in range(2)]
        w_hi = [at(f"w_hi{s}", [P, KH * CW], F32R, hi_at[s]) for s in range(2)]
        w_lo = [at(f"w_lo{s}", [P, KH * CW], F32R, lo_at[s]) for s in range(2)]

        X_AT, XH_AT, XL_AT = region(DK * TB), region(DK * TB), region(DK * TB)
        x = at("x_res", [P, DK, T], F32, X_AT)
        xh = at("xh", [P, DK, T], F32R, XH_AT)
        xl = at("xl", [P, DK, T], F32R, XL_AT)
        fo = at("fo", [P, DK, T], F32, XH_AT)
        sq_norm = at("sq_norm", [P, T], F32, XL_AT)

        HB = region(2 * FK * TB)

        tails = [b + DK * CW * 4 for b in (raw_at[0], raw_at[1], hi_at[0], hi_at[1], lo_at[0], lo_at[1])]
        rs_row = at("rs_row", [P, T], F32, tails[5])
        sqx = [at(f"sqx{i}", [P, T], F32, tails[1 + i]) for i in range(2)]
        cv_sum = [at(f"cv_sum{e}", [P, T], F32, tails[e]) for e in (1, 2)]
        cv_prod = [at("cv_prod0", [P, T], F32, tails[3]), at("cv_prod1", [P, T], F32, tails[4]),
                   at("cv_prod2", [P, T], F32, tails[0]), None]

        def slot(name, s, shape, dt):
            return at(name, shape, dt, HB + s * TB)

        hh = slot("hh", 0, [P, FK, T], F32R)
        hl = slot("hl", FK, [P, FK, T], F32R)
        hs = slot("hs", FK, [P, FK, T], F32)
        x_tok = slot("x_tok", 0, [P, SC, D], F32)
        par_rows = slot("par_rows", 8, [P, 4, P], F32)
        u = slot("u", 0, [P, DK, T], F32)
        xbc = slot("xbc", 8, [P, XT, T], F32)
        z = slot("z", 20, [P, DK, T], F32)
        x_dt = slot("x_dt", 28, [P, SC, D_SSM], F32)
        b_tok = slot("b_tok", 36, [P, GROUPS, SC, STATE], F32)
        g_mask = slot("g_mask", 38, [P, GROUPS, SC, P], F32)
        cv_prod[3] = slot("cv_prod3", 40, [P, T], F32)
        dtw = slot("dtw", 42, [P, DK, HEADS], F32)
        dtwh = at("dtwh", [P, DK, HEADS], F32R, HB + 42 * TB + 512)
        dtwl = at("dtwl", [P, DK, HEADS], F32R, HB + 42 * TB + 1024)
        tri_r = at("tri_r", [P, P], F32R, HB + 43 * TB)
        da_hi = at("da_hi", [P, SC * HEADS], F32R, HB + 43 * TB + 512)
        da_lo = at("da_lo", [P, SC * HEADS], F32R, HB + 43 * TB + 768)
        sq_y = [slot(f"sq_y{i}", 41 + i, [P, T], F32) for i in range(2)]
        hst = at("hst", [P, SC - 1, D_SSM], F32, XH_AT)
        x_dec = at("x_dec", [P, 2, T], F32, XH_AT + 6 * TB)
        l_t = at("l_t", [P, 2, T], F32, XL_AT)
        e_t = at("e_t", [P, 2, T], F32, XL_AT + 2 * TB)
        m_t = at("m_t", [P, 4, T], F32, XL_AT + 4 * TB)
        ysh = slot("ysh", 8, [P, DK, T], F32R)
        ysl = slot("ysl", 20, [P, DK, T], F32R)
        ych = slot("ych", 28, [P, DK, T], F32R)
        ycl = slot("ycl", 0, [P, DK, T], F32R)

        def small(name, shape):
            n = 4
            for d in shape[1:]:
                n *= d
            return at(name, shape, F32, region(n))

        par = small("par", [P, NPAR])
        ones = small("ones", [P, P])
        tri = small("tri", [P, P])
        ident = small("ident", [P, P])
        d_col = small("d_col", [P, DK])
        eps = small("eps", [P, 1])
        spare = small("spare", [P, 2])
        dtb = small("dtb", [P, HEADS])
        alog = small("alog", [P, HEADS])
        dt_tok = small("dt_tok", [P, SC, HEADS])
        da_tok = small("da_tok", [P, SC, HEADS])
        t_abs = small("t_abs", [P, SC, HEADS])
        acs = small("acs", [P, SC, HEADS])
        dend = small("dend", [P, SC, HEADS])
        wdec = small("wdec", [P, SC, HEADS])

        rms = small("rms", [P, SC])
        rinv = small("rinv", [P, SC])
        bank = [nc.alloc_psum_tensor(f"bank{b}", [P, T], F32) for b in range(8)]

        def col(name, k):
            c = COL[name] + k
            return par[:, c:c + 1]

        raw_in = [sem(f"raw_in{s}") for s in range(2)]
        hi_done = sem("hi_done")
        lo_done = sem("lo_done")
        w_used = sem("w_used")
        x_in = [sem(f"x_in{c}") for c in range(SC)]
        par_in = sem("par_in")
        small_in = sem("small_in")
        dtw_in = sem("dtw_in")
        consts_cleared = sem("consts_cleared")
        consts = sem("consts")
        par_t = sem("par_t")
        par_ok = sem("par_ok")
        x_turned = sem("x_turned")
        x_ready = sem("x_ready")
        tile_done = [sem(f"tile_done{s}") for s in range(2)]
        acc_done = sem("acc_done")
        gate_v = sem("gate_v")
        silu_done = sem("silu_done")
        up_v = sem("up_v")
        hh_done = sem("hh_done")
        hl_done = sem("hl_done")
        fo_done = sem("fo_done")
        out_turned = sem("out_turned")
        out_copied = [sem(f"out_copied{h}") for h in range(2)]
        stored = sem("stored")

        class Norm:

            def __init__(self, n, pre=False, post=False, split=False):
                self.sq = sem(f"{n}_sq")
                self.sum = sem(f"{n}_sum")
                self.root = sem(f"{n}_root")
                self.inv = sem(f"{n}_inv")
                self.row = sem(f"{n}_row")
                if pre or split:
                    self.hi = sem(f"{n}_hi")
                    self.lo = sem(f"{n}_lo")
                if pre:
                    self.rs = sem(f"{n}_rs")
                if post or split:
                    self.val = sem(f"{n}_val")
                if post:
                    self.add = sem(f"{n}_add")
                    self.a = sem(f"{n}_a")

        pre1, prem, pre2 = (Norm(n, pre=True) for n in ("pre1", "prem", "pre2"))
        post1, postm, post2 = (Norm(n, post=True) for n in ("post1", "postm", "post2"))
        ssdn = [Norm(f"ssdn{g}", split=True) for g in range(GROUPS)]
        lnn = Norm("lnn", split=True)

        dtw_hi = sem("dtw_hi")
        dtw_lo = sem("dtw_lo")
        dt_raw = sem("dt_raw")
        dt_v = sem("dt_v")
        dt_s = sem("dt_s")
        acs_t = sem("acs_t")
        acs_v = sem("acs_v")
        acs_s = sem("acs_s")
        ga_v = sem("ga_v")
        gg_v = sem("gg_v")
        sg_done = sem("sg_done")
        u_done = sem("u_done")
        cv_start = sem("cv_start")
        cv_step = sem("cv_step")
        cv_out = sem("cv_out")
        cp_start = sem("cp_start")
        cp_prod = sem("cp_prod")
        cp_step = sem("cp_step")
        cp_out = sem("cp_out")
        xs_v = sem("xs_v")
        cb_start = sem("cb_start")
        cb_step = sem("cb_step")
        xbc_done = sem("xbc_done")
        zs_v = sem("zs_v")
        z_done = sem("z_done")
        bt_t = sem("bt_t")
        bt_c = sem("bt_c")
        cbm_t = sem("cbm_t")
        cbm_v = sem("cbm_v")
        xt_t = sem("xt_t")
        xt_v = sem("xt_v")
        xdec_v = sem("xdec_v")
        st_t = sem("st_t")
        st_v = sem("st_v")
        st_m = sem("st_m")
        da_s = sem("da_s")
        da_v = sem("da_v")
        r_t = sem("r_t")
        seg_s = sem("seg_s")
        l_s = sem("l_s")
        e_s = sem("e_s")
        m_v = sem("m_v")
        off_t = sem("off_t")
        off_v = sem("off_v")
        diag_t = sem("diag_t")
        y_a = sem("y_a")
        y_d = sem("y_d")
        y_v = sem("y_v")
        mu_t = sem("mu_t")
        mu_s = sem("mu_s")
        mu_row = sem("mu_row")
        cen_v = sem("cen_v")
        ln_act = sem("ln_act")

        def wait_tile(eng, b, it, pr):
            if b % 2 == 0:
                eng.wait_ge(tile_done[b // 2], pr + 1)
            else:
                eng.wait_ge(w_used, it * 2 + (1 + b // 2))

        def wait_out(eng, t, it, ac):
            if t == 0:
                eng.wait_ge(acc_done, ac + 1)
            else:
                eng.wait_ge(w_used, it * 2 + 2)

        block = ctx.enter_context(nc.Block())

        @block.sync
        def _(sp):
            for c in range(SC):
                sp.dma_start(x_tok[:, c, :], a["x"][0, c * P:(c + 1) * P, :]).then_inc(x_in[c], 16)

            def load(it, srcs, first=False):
                for s in range(2):
                    if not first:
                        sp.wait_ge(lo_done, it * 2 + (s - 1))
                    kn = srcs[s].shape[1]
                    sp.dma_start(w_raw[s][:, 0:kn * CW].rearrange("p (k n) -> p k n", k=kn),
                                 srcs[s]).then_inc(raw_in[s], 16)

            def ffn(n, it0, first):
                wg, wu, wd = (a[f"ffn{n}_w_{m}"][0].rearrange("(k p) f -> p k f", p=P) for m in ("gate", "up", "down"))
                if first:
                    load(0, [wg[:, :, 0:CW], wu[:, :, 0:CW]], True)
                with sp.Fori(1 if first else 0, FK // 2) as i:
                    load(i + it0, [wg[:, :, bass.ds(i * CW, CW)], wu[:, :, bass.ds(i * CW, CW)]])
                with sp.Fori(0, DK // 2) as m:
                    load(m + (it0 + FK // 2), [wd[:, h * KH:(h + 1) * KH, bass.ds(m * CW, CW)] for h in range(2)])

            ffn(1, IT_GU1, True)
            w_in = a["w_in"][0].rearrange("(k p) f -> p k f", p=P)
            with sp.Fori(0, DK // 2) as i:
                load(i + IT_GLU, [w_in[:, :, bass.ds(i * CW + (GLU0 + j * D_CONV), CW)] for j in range(2)])
            with sp.Fori(0, XT // 4) as i:
                load(i + IT_XBC, [w_in[:, :, bass.ds(i * (2 * CW) + (XBC0 + j * CW), CW)] for j in range(2)])
            with sp.Fori(0, DK // 4) as i:
                load(i + IT_Z, [w_in[:, :, bass.ds(i * (2 * CW) + (Z0 + j * CW), CW)] for j in range(2)])
            w_out = a["w_out"][0].rearrange("(k p) f -> p k f", p=P)
            for i in range(len(OUT_CHUNKS) // 2):
                load(IT_OUT + i, [w_out[:, h * DK:(h + 1) * DK, m * CW:(m + 1) * CW] for h, m in OUT_CHUNKS[2 * i:2 * i + 2]])
            ffn(2, IT_GU2, False)
            for h in range(2):
                for c in range(SC):
                    sp.wait_ge(out_copied[h], c + 1)
                    sp.dma_start(out[0, c * P:(c + 1) * P, h * T:(h + 1) * T], x_tok[:, c, h * T:(h + 1) * T]).then_inc(stored, 16)
            sp.wait_ge(stored, 16 * 2 * SC)

        @block.gpsimd
        def _(pool):
            pool.memset(ident[:, :], 0.0).then_inc(consts_cleared, 1)
            pool.memset(tri[:, :], 1.0).then_inc(consts_cleared, 1)
            pool.memset(ones[:, :], 1.0).then_inc(consts, 1)
            pool.memset(eps[:, :], EPS).then_inc(consts, 1)
            pool.wait_ge(consts_cleared, 2)
            pool.affine_select(out=ident[:, :], in_=ident[:, :], compare_op=ALU.not_equal, fill=1.0, base=0,
                               pattern=[[-1, P]], channel_multiplier=1).then_inc(consts, 1)
            pool.affine_select(out=tri[:, :], in_=tri[:, :], compare_op=ALU.is_ge, fill=0.0, base=0,
                               pattern=[[1, P]], channel_multiplier=-1).then_inc(consts, 1)

            def rest(s, it, kn, first=False):
                pool.wait_ge(hi_done, it * 2 + (s + 1))
                if not first:
                    pool.wait_ge(w_used, it * 2 + (s - 1))
                pool.tensor_tensor(w_lo[s][:, 0:kn * CW], w_raw[s][:, 0:kn * CW], w_hi[s][:, 0:kn * CW].bitcast(F32),
                                   ALU.subtract).then_inc(lo_done, 1)

            def rests(it, kn, first=False):
                for s in range(2):
                    rest(s, it, kn, first)

            def conv(begin, end):
                for n in range(begin, end):
                    q, back = n // STEPS, n % STEPS + 1
                    for e in range(2):
                        if back == 1:
                            pool.wait_ge(cp_start, 2 * q + e + 1)
                        else:
                            pool.wait_ge(cp_step, 2 * n + e - 1)
                        pool.wait_ge(cp_prod, 2 * n + e + 1)
                        pool.tensor_tensor(cv_sum[e][:, back:], cv_sum[e][:, back:], cv_prod[(2 * n + e) % 4][:, back:],
                                           ALU.add).then_inc(cp_step, 1)

            rests(0, DK, True)
            with pool.Fori(1, IT_DOWN1) as i:
                rests(i, DK)
            def down_rests(it0, n, end):
                rest(0, it0, KH)
                pool.wait_ge(hl_done, (n + 1) * FK)
                rest(1, it0, KH)
                with pool.Fori(it0 + 1, end) as i:
                    rests(i, KH)
            down_rests(IT_DOWN1, 0, IT_GLU)
            rests(IT_GLU, DK)
            for n in range(IT_OUT - IT_GLU):
                begin, end = POOL_AT[n], POOL_AT[n + 1]
                mid = (begin + end) // 2
                conv(begin, mid)
                rest(0, IT_GLU + n + 1, DK)
                conv(mid, end)
                rest(1, IT_GLU + n + 1, DK)
            conv(POOL_AT[-2], POOL_AT[-1])
            with pool.Fori(IT_OUT + 1, IT_DOWN2) as i:
                rests(i, DK)
            down_rests(IT_DOWN2, 1, IT_END)

        @block.scalar
        def _(act):
            row = 0
            for name, k in VECS:
                act.dma_start(par_rows[row:row + k, 0, :], a[name].rearrange("l (k p) -> (l k) p", p=P)).then_inc(par_in, 16)
                row += k
            act.dma_start(par_rows[0:STAPS * XT, 1, :],
                          a["ssd_conv_w"].rearrange("l j (t p) -> (l j t) p", p=P)).then_inc(par_in, 16)
            cw = a["conf_dw_w"].rearrange("l j (t p) -> (l j t) p", p=P)
            for h in range(2):
                act.dma_start(par_rows[0:HALF_ROWS, 2 + h, :], cw[h * HALF_ROWS:(h + 1) * HALF_ROWS, :]).then_inc(par_in, 16)
            act.dma_start(dtb[:, :], a["dt_bias"].to_broadcast([P, HEADS])).then_inc(small_in, 16)
            act.dma_start(alog[:, :], a["a_log"].to_broadcast([P, HEADS])).then_inc(small_in, 16)
            dsk = a["d_skip"].rearrange("l (t h) -> l h t", h=2)
            with nc.allow_non_contiguous_dma(reason="16 values"):
                for h in range(2):
                    act.dma_start(d_col[h * HD:(h + 1) * HD, :], dsk[:, h, :].to_broadcast([HD, DK])).then_inc(small_in, 16)

            def round_w(s, it, kn, first=False):
                act.wait_ge(raw_in[s], it * 16 + 16)
                if not first:
                    act.wait_ge(w_used, it * 2 + (s - 1))
                act.activation(w_hi[s][:, 0:kn * CW], w_raw[s][:, 0:kn * CW], ACT.Copy).then_inc(hi_done, 1)

            def table(f):
                act.activation(spare[:, 0:1], spare[:, 1:2], f)

            def root(nm, b, n, sums):
                act.wait_ge(nm.sum, sums)
                act.activation(rms[:, :], bank[b][:, 0:SC], ACT.Sqrt, bias=eps[:, 0:1], scale=1.0 / n).then_inc(nm.root, 1)

            def square(nm, k, src, ring):
                if k >= 2:
                    act.wait_ge(nm.sum, k - 1)
                act.activation(ring[k % 2][:, :], src, ACT.Square).then_inc(nm.sq, 1)

            def pre_norm(nm, gain, ready):
                table(ACT.Sqrt)
                for k in range(DK):
                    ready(k)
                    act.activation(xh[:, k, :], x[:, k, :], ACT.Copy, scale=col(gain, k)).then_inc(nm.hi, 1)
                    square(nm, k, x[:, k, :], sqx)
                root(nm, 7, D, DK)

            def gate_up(n, it0, pr0):
                def hidden(i, kn):
                    tl = i * 2 + n * FK
                    for t in range(2):
                        act.wait_ge(gate_v, tl + (t + 1))
                        act.activation(hs[:, i * 2 + t, :], bank[t][:, :], ACT.Silu).then_inc(silu_done, 1)
                        if t == 0:
                            round_w(0, i + (it0 + 1), kn)
                    for t in range(2):
                        if t:
                            round_w(1, i + (it0 + 1), kn)
                        act.wait_ge(up_v, 2 * tl + (2 * t + 2))
                        act.activation(hh[:, i * 2 + t, :], bank[2 + t][:, :], ACT.Copy).then_inc(hh_done, 1)
                table(ACT.Silu)
                with act.Fori(0, FK // 2 - 1) as i:
                    hidden(i, DK)
                hidden(FK // 2 - 1, KH)

            def take(nm, m, b, before):
                act.activation(fo[:, m, :], bank[b][:, :], ACT.Copy).then_inc(fo_done, 1)
                act.wait_ge(fo_done, m + (before + 1))
                act.activation(bank[b][:, :], bank[b][:, :], ACT.Square).then_inc(nm.sq, 1)

            def take_down(nm, it0, ac0, kn_next):
                def pair(i, kn):
                    if kn:
                        round_w(0, i + (it0 + 1), kn)
                    wait_out(act, 0, i + it0, i + ac0)
                    take(nm, i * 2, 4, 2 * ac0)
                    if kn:
                        round_w(1, i + (it0 + 1), kn)
                    wait_out(act, 1, i + it0, i + ac0)
                    take(nm, i * 2 + 1, 5, 2 * ac0)
                with act.Fori(0, DK // 2 - 1) as i:
                    pair(i, KH)
                table(ACT.Sqrt)
                pair(DK // 2 - 1, kn_next)
                root(nm, 6, D, 1)

            def square_y(q):
                g, k = q // (DK // GROUPS), q % (DK // GROUPS)
                act.wait_ge(y_v, q + 1)
                if q >= 2:
                    qq = q - 2
                    act.wait_ge(ssdn[qq // (DK // GROUPS)].sum, qq % (DK // GROUPS) + 1)
                act.activation(sq_y[q % 2][:, :], z[:, q, :], ACT.Square).then_inc(ssdn[g].sq, 1)

            def round_y(g):
                for k in range(DK // GROUPS):
                    act.wait_ge(ssdn[g].val, k + 1)
                    act.activation(ysh[:, 4 * g + k, :], z[:, 4 * g + k, :], ACT.Copy).then_inc(ssdn[g].hi, 1)

            for s in range(2):
                round_w(s, 0, DK, True)
            act.wait_ge(consts, 4)
            act.wait_ge(par_ok, 4)
            pre_norm(pre1, "ffn1_pre_g", lambda k: act.wait_ge(x_ready, k + 1))
            gate_up(0, IT_GU1, PR_GU1)
            take_down(post1, IT_DOWN1, AC_DOWN1, DK)
            act.wait_ge(w_used, 2 * IT_GLU)
            act.dma_start(dtw[:, :, :], a["w_in"][0].rearrange("(k p) f -> p k f", p=P)[:, :, DT0:DT0 + HEADS]).then_inc(dtw_in, 16)
            act.activation(tri_r[:, :], tri[:, :], ACT.Copy).then_inc(da_s, 1)
            pre_norm(prem, "mix_pre_g", lambda k: act.wait_ge(post1.val, k + 1))
            act.wait_ge(dtw_in, 16)
            act.activation(dtwh[:, :, :], dtw[:, :, :], ACT.Copy).then_inc(dtw_hi, 1)

            def conv_turns(n):
                for step in range(DVE_AT[n], DVE_AT[n + 1]):
                    q, back = step // STEPS, step % STEPS + 1
                    for e in range(2):
                        c = 2 * (POOL_PAIRS + q) + e
                        if back == 1:
                            act.wait_ge(u_done, c + 1)
                            if q:
                                act.wait_ge(cv_out, 2 * q - 1 + e)
                            act.activation(bank[4 + e][:, :], u[:, c, :], ACT.Identity, bias=col("conf_dw_b", c),
                                           scale=col("conf_dw_w", STEPS * DK + c)).then_inc(cv_start, 1)
                        if back == STEPS:
                            act.wait_ge(cv_step, 2 * step + 1 + e)
                            act.activation(u[:, c, :], bank[4 + e][:, :], ACT.Copy).then_inc(cv_out, 1)

            def products(begin, end):
                for n in range(begin, end):
                    q, back = n // STEPS, n % STEPS + 1
                    for e in range(2):
                        c, m = 2 * q + e, 2 * n + e
                        if back == 1:
                            if q:
                                conv_close(q - 1, e)
                                act.wait_ge(cp_out, 2 * q - 1 + e)
                            act.wait_ge(u_done, c + 1)
                            act.activation(cv_sum[e][:, :], u[:, c, :], ACT.Identity, bias=col("conf_dw_b", c),
                                           scale=col("conf_dw_w", STEPS * DK + c)).then_inc(cp_start, 1)
                        if m >= 4:
                            act.wait_ge(cp_step, m - 3)
                        act.activation(cv_prod[m % 4][:, back:], u[:, c, 0:T - back], ACT.Copy,
                                       scale=col("conf_dw_w", (STEPS - back) * DK + c)).then_inc(cp_prod, 1)

            def conv_close(q, e):
                act.wait_ge(cp_step, 2 * (q + 1) * STEPS - 1 + e)
                act.activation(u[:, 2 * q + e, :], cv_sum[e][:, :], ACT.Copy).then_inc(cp_out, 1)

            def share(n, part, parts):
                begin, count = POOL_AT[n], POOL_STEPS[n]
                products(begin + count * part // parts, begin + count * (part + 1) // parts)

            table(ACT.Sigmoid)
            for i in range(DK // 2):
                share(i, 0, 3)
                round_w(0, IT_GLU + i + 1, DK)
                share(i, 1, 3)
                for t in range(2):
                    if t:
                        share(i, 2, 3)
                        round_w(1, IT_GLU + i + 1, DK)
                    c = 2 * i + t
                    act.wait_ge(gg_v, c + 1)
                    act.activation(bank[2 + t][:, :], bank[2 + t][:, :], ACT.Sigmoid, bias=col("b_glu", DK + c)).then_inc(sg_done, 1)
                conv_turns(i)
            act.wait_ge(dt_v, 4)
            act.activation(t_abs[:, :, :], dt_tok[:, :, :], ACT.Abs).then_inc(dt_s, 1)
            act.wait_ge(dt_s, 1)
            act.activation(t_abs[:, :, :], t_abs[:, :, :], ACT.Exp, scale=-1.0).then_inc(dt_s, 1)
            act.wait_ge(dt_s, 2)
            act.activation(t_abs[:, :, :], t_abs[:, :, :], ACT.Ln, bias=1.0).then_inc(dt_s, 1)
            act.wait_ge(small_in, 64)
            act.activation(alog[:, :], alog[:, :], ACT.Exp).then_inc(dt_s, 1)
            act.wait_ge(dt_v, 6)
            act.activation(da_hi[:, :], da_tok[:, :, :].rearrange("p c h -> p (c h)"), ACT.Copy).then_inc(da_s, 1)
            for i in range(XT // 4):
                n = DK // 2 + i

                def newest(b):
                    c = 4 * i + b
                    act.wait_ge(xs_v, c + 1)
                    act.activation(xbc[:, c, :], bank[b][:, :], ACT.Identity, bias=col("ssd_conv_b", c),
                                   scale=col("ssd_conv_w", (STAPS - 1) * XT + c)).then_inc(cb_start, 1)

                def finish(b):
                    c = 4 * i + b
                    act.wait_ge(cb_step, short_steps(c))
                    act.activation(xbc[:, c, :], xbc[:, c, :], ACT.Silu).then_inc(xbc_done, 1)
                table(ACT.Silu)
                share(n, 0, 4)
                newest(0)
                share(n, 1, 4)
                newest(1)
                round_w(0, IT_XBC + i + 1, DK)
                share(n, 2, 4)
                finish(0)
                finish(1)
                newest(2)
                share(n, 3, 4)
                round_w(1, IT_XBC + i + 1, DK)
                newest(3)
                finish(2)
                finish(3)
                conv_turns(n)
            act.wait_ge(acs_v, 2)
            act.activation(wdec[:, :, :], wdec[:, :, :], ACT.Exp).then_inc(acs_s, 1)
            act.activation(dend[:, :, :].rearrange("p c h -> p (c h)"), bank[6][:, 64:128], ACT.Exp).then_inc(acs_s, 1)
            table(ACT.Silu)
            for i in range(DK // 4):
                n = DK // 2 + XT // 4 + i
                for b in range(4):
                    if b:
                        share(n, b - 1, 3)
                    act.wait_ge(zs_v, 4 * i + b + 1)
                    act.activation(z[:, 4 * i + b, :], bank[b][:, :], ACT.Silu).then_inc(z_done, 1)
                    if b == 0:
                        round_w(0, IT_Z + i + 1, DK)
                    if b == 2:
                        round_w(1, IT_Z + i + 1, DK)
                if i == 0:
                    for g in range(GROUPS):
                        act.wait_ge(bt_t, g + 1)
                        act.activation(b_tok[:, g, :, :].rearrange("p c n -> p (c n)"), bank[6 + g][:, :], ACT.Copy).then_inc(bt_c, 1)
                conv_turns(n)
            last = len(POOL_STEPS) - 1
            for q in range(DK):
                act.wait_ge(r_t, q + 1)
                for e in range(2):
                    h = 2 * q + e
                    if q:
                        act.wait_ge(m_v, h - 1)
                    for c in range(SC):
                        act.activation(l_t[:, e, c * P:(c + 1) * P], bank[e][:, c * P:(c + 1) * P], ACT.Relu,
                                       bias=acs[:, c, h:h + 1], scale=-1.0).then_inc(seg_s, 1)
                if q >= 2:
                    act.wait_ge(y_a, q - 1)
                act.activation(e_t[:, q % 2, :], bank[2][:, :], ACT.Exp).then_inc(e_s, 1)
                for e in range(2):
                    act.wait_ge(seg_s, SC * (2 * q + e + 1))
                    act.activation(l_t[:, e, :], l_t[:, e, :], ACT.Exp, scale=-1.0).then_inc(l_s, 1)
                share(last, q, DK)
                if q:
                    square_y(q - 1)
                if q == DK // 2 + 1:
                    root(ssdn[0], 3, D_SSM // GROUPS, DK // GROUPS)
                if q == DK - 1:
                    round_y(0)
            square_y(DK - 1)
            conv_turns(last)
            for e in range(2):
                conv_close(POOL_PAIRS - 1, e)
            table(ACT.Sqrt)
            root(ssdn[1], 3, D_SSM // GROUPS, DK // GROUPS)
            act.wait_ge(ssdn[1].inv, 1)
            act.wait_ge(mu_t, 1)
            act.activation(rms[:, :], bank[6][:, 0:SC], ACT.Copy, scale=-1.0 / D_CONV).then_inc(mu_s, 1)
            round_y(1)
            for c in range(DK):
                act.wait_ge(cen_v, c + 1)
                square(lnn, c, u[:, c, :], sq_y)
            root(lnn, 7, D_CONV, DK)
            round_w(0, IT_OUT + 1, DK)
            table(ACT.Silu)
            for c in range(DK):
                act.wait_ge(lnn.val, c + 1)
                act.activation(u[:, c, :], u[:, c, :], ACT.Silu, bias=col("conf_ln_b", c)).then_inc(ln_act, 1)
                act.wait_ge(ln_act, c + 1)
                act.activation(ych[:, c, :], u[:, c, :], ACT.Copy).then_inc(lnn.hi, 1)

            for j, (half, m) in enumerate(OUT_CHUNKS):
                if j:
                    round_w(j % 2, IT_OUT + j // 2 + 1, DK)
                if half:
                    for t in range(2):
                        if t:
                            act.wait_ge(w_used, 2 * IT_OUT + j + 1)
                        else:
                            act.wait_ge(acc_done, AC_OUT + m + 1)
                        if j == len(OUT_CHUNKS) - 1 and t:
                            table(ACT.Sqrt)
                        take(postm, 2 * m + t, out_bank(2 * m + t), 2 * AC_OUT)
            root(postm, 6, D, 1)
            pre_norm(pre2, "ffn2_pre_g", lambda k: act.wait_ge(postm.val, k + 1))
            gate_up(1, IT_GU2, PR_GU2)
            take_down(post2, IT_DOWN2, AC_DOWN2, 0)
            for c in range(SC):
                act.wait_ge(out_turned, c + 1)
                act.activation(x_tok[:, c, 0:T], bank[c][:, :], ACT.Copy).then_inc(out_copied[0], 1)

        @block.vector
        def _(dve):
            def invert(nm):
                dve.wait_ge(nm.root, 1)
                dve.reciprocal(rinv[:, :], rms[:, :]).then_inc(nm.inv, 1)

            def keep_row(nm):
                dve.wait_ge(nm.row, 1)
                dve.tensor_copy(rs_row[:, :], bank[7][:, :]).then_inc(nm.rs, 1)
                dve.wait_ge(nm.rs, 1)

            def rest_x(nm, gain, k):
                dve.wait_ge(nm.hi, k + 1)
                dve.scalar_tensor_tensor(out=xl[:, k, :], in0=x[:, k, :], scalar=col(gain, k), in1=xh[:, k, :].bitcast(F32),
                                         op0=ALU.mult, op1=ALU.subtract).then_inc(nm.lo, 1)

            def gate_up(n, it0, pr0):
                with dve.Fori(0, FK // 2) as i:
                    tl = i * 2 + n * FK
                    for t in range(2):
                        wait_tile(dve, t, i + it0, i + pr0)
                        dve.tensor_tensor(bank[t][:, :], bank[t][:, :], rs_row[:, :], ALU.mult).then_inc(gate_v, 1)
                    for t in range(2):
                        dve.wait_ge(silu_done, tl + (t + 1))
                        wait_tile(dve, 2 + t, i + it0, i + pr0)
                        dve.tensor_tensor(bank[2 + t][:, :], hs[:, i * 2 + t, :], bank[2 + t][:, :], ALU.mult).then_inc(up_v, 1)
                        dve.wait_ge(up_v, 2 * tl + (2 * t + 1))
                        dve.tensor_tensor(bank[2 + t][:, :], bank[2 + t][:, :], rs_row[:, :], ALU.mult).then_inc(up_v, 1)
                    for t in range(2):
                        dve.wait_ge(hh_done, tl + (t + 1))
                        dve.tensor_tensor(hl[:, i * 2 + t, :], bank[2 + t][:, :], hh[:, i * 2 + t, :].bitcast(F32),
                                          ALU.subtract).then_inc(hl_done, 1)

            def clear(nm):
                dve.memset(sq_norm[:, :], 0.0).then_inc(nm.add, 1)

            def add_square(nm, m, b):
                dve.wait_ge(nm.sq, m + 1)
                dve.wait_ge(nm.add, m + 1)
                dve.tensor_tensor(sq_norm[:, :], sq_norm[:, :], bank[b][:, :], ALU.add).then_inc(nm.add, 1)

            def add_down(nm):
                with dve.Fori(0, DK // 2) as i:
                    for t in range(2):
                        add_square(nm, i * 2 + t, 4 + t)

            def post_norm(nm, gain, after):
                invert(nm)
                dve.wait_ge(nm.row, 1)
                for k in range(DK + 2):
                    if k < DK:
                        dve.tensor_tensor(fo[:, k, :], fo[:, k, :], bank[6][:, :], ALU.mult).then_inc(nm.a, 1)
                    if 1 <= k <= DK:
                        dve.wait_ge(nm.a, k)
                        dve.scalar_tensor_tensor(out=x[:, k - 1, :], in0=fo[:, k - 1, :], scalar=col(gain, k - 1),
                                                 in1=x[:, k - 1, :], op0=ALU.mult, op1=ALU.add).then_inc(nm.val, 1)
                    if k >= 2:
                        after(k - 2)

            dve.memset(spare[:, :], 0.0).then_inc(par_ok, 1)
            dve.wait_ge(par_t, 1)
            dve.tensor_copy(par[:, :], bank[7][:, 0:NPAR]).then_inc(par_ok, 1)
            dve.wait_ge(par_ok, 2)
            for name in ("ffn1_post_g", "ffn2_post_g"):
                g = par[:, COL[name]:COL[name] + DK]
                dve.tensor_scalar(g, g, 0.5, None, ALU.mult).then_inc(par_ok, 1)
            dve.wait_ge(par_ok, 4)
            for k in range(DK + 2):
                if k < DK:
                    dve.wait_ge(x_turned, k + 1)
                    dve.tensor_copy(x[:, k, :], bank[turn_bank(k)][:, :]).then_inc(x_ready, 1)
                if k >= 2:
                    rest_x(pre1, "ffn1_pre_g", k - 2)
            invert(pre1)
            keep_row(pre1)
            gate_up(0, IT_GU1, PR_GU1)
            dve.wait_ge(w_used, 2 * IT_DOWN1)
            clear(post1)
            add_down(post1)
            post_norm(post1, "ffn1_post_g", lambda k: rest_x(prem, "mix_pre_g", k))
            invert(prem)
            dve.wait_ge(dtw_hi, 1)
            dve.tensor_tensor(dtwl[:, :, :], dtw[:, :, :], dtwh[:, :, :].bitcast(F32), ALU.subtract).then_inc(dtw_lo, 1)
            keep_row(prem)

            def conv(n):
                for step in range(DVE_AT[n], DVE_AT[n + 1]):
                    q, back = step // STEPS, step % STEPS + 1
                    for e in range(2):
                        c = 2 * (POOL_PAIRS + q) + e
                        if back == 1:
                            dve.wait_ge(cv_start, 2 * q + e + 1)
                        else:
                            dve.wait_ge(cv_step, 2 * step + e - 1)
                        dve.scalar_tensor_tensor(out=bank[4 + e][:, back:], in0=u[:, c, 0:T - back],
                                                 scalar=col("conf_dw_w", (STEPS - back) * DK + c),
                                                 in1=bank[4 + e][:, back:], op0=ALU.mult, op1=ALU.add).then_inc(cv_step, 1)

            for i in range(DK // 2):
                for t in range(2):
                    wait_tile(dve, t, IT_GLU + i, PR_GLU + i)
                    dve.tensor_tensor(u[:, 2 * i + t, :], bank[t][:, :], rs_row[:, :], ALU.mult).then_inc(ga_v, 1)
                if i == 0:
                    dve.wait_ge(dt_raw, 1)
                    dve.wait_ge(small_in, 64)
                    for c in range(SC):
                        dve.scalar_tensor_tensor(out=dt_tok[:, c, :], in0=bank[6][:, c * HEADS:(c + 1) * HEADS],
                                                 scalar=rinv[:, c:c + 1], in1=dtb[:, :],
                                                 op0=ALU.mult, op1=ALU.add).then_inc(dt_v, 1)
                for t in range(2):
                    wait_tile(dve, 2 + t, IT_GLU + i, PR_GLU + i)
                    dve.tensor_tensor(bank[2 + t][:, :], bank[2 + t][:, :], rs_row[:, :], ALU.mult).then_inc(gg_v, 1)
                for t in range(2):
                    c = 2 * i + t
                    dve.wait_ge(ga_v, c + 1)
                    dve.wait_ge(sg_done, c + 1)
                    dve.scalar_tensor_tensor(out=u[:, c, :], in0=u[:, c, :], scalar=col("b_glu", c), in1=bank[2 + t][:, :],
                                             op0=ALU.add, op1=ALU.mult).then_inc(u_done, 1)
                if i == DK // 2 - 1:
                    dve.wait_ge(dt_s, 4)
                    dve.scalar_tensor_tensor(out=dt_tok[:, :, :], in0=dt_tok[:, :, :], scalar=0.0, in1=t_abs[:, :, :],
                                             op0=ALU.max, op1=ALU.add).then_inc(dt_v, 1)
                    dve.wait_ge(dt_v, SC + 1)
                    dve.scalar_tensor_tensor(out=da_tok[:, :, :], in0=dt_tok[:, :, :], scalar=-1.0,
                                             in1=alog[:, :].unsqueeze(1).to_broadcast([P, SC, HEADS]),
                                             op0=ALU.mult, op1=ALU.mult).then_inc(dt_v, 1)
                    dve.wait_ge(dt_v, SC + 2)
                    dve.wait_ge(da_s, 2)
                    dve.tensor_tensor(da_lo[:, :], da_tok[:, :, :].rearrange("p c h -> p (c h)"), da_hi[:, :].bitcast(F32),
                                      ALU.subtract).then_inc(da_v, 1)
                conv(i)
            for i in range(XT // 4):
                for b0 in (0, 2):
                    for e in range(2):
                        b = b0 + e
                        wait_tile(dve, b, IT_XBC + i, PR_XBC + i)
                        dve.tensor_tensor(bank[b][:, :], bank[b][:, :], rs_row[:, :], ALU.mult).then_inc(xs_v, 1)
                    for s in range(1, STAPS):
                        for e in range(2):
                            b = b0 + e
                            c = 4 * i + b
                            done = short_steps(c) - 1 - 2 * (STAPS - 1 - s)
                            if s == 1:
                                dve.wait_ge(cb_start, c + 1)
                            else:
                                dve.wait_ge(cb_step, done - 1)
                            dve.scalar_tensor_tensor(out=xbc[:, c, s:], in0=bank[b][:, 0:T - s],
                                                     scalar=col("ssd_conv_w", (STAPS - 1 - s) * XT + c),
                                                     in1=xbc[:, c, s:], op0=ALU.mult, op1=ALU.add).then_inc(cb_step, 1)
                conv(DK // 2 + i)
                if i == 0:
                    dve.wait_ge(acs_t, 1)
                    dve.tensor_copy(acs[:, :, :].rearrange("p c h -> p (c h)"), bank[6][:, 0:64]).then_inc(acs_v, 1)
                    dve.wait_ge(acs_v, 1)
                    dve.tensor_tensor(wdec[:, :, :].rearrange("p c h -> p (c h)"), bank[6][:, 64:128],
                                      acs[:, :, :].rearrange("p c h -> p (c h)"), ALU.subtract).then_inc(acs_v, 1)

            def scale_z(c):
                wait_tile(dve, c % 4, IT_Z + c // 4, PR_Z + c // 4)
                dve.tensor_tensor(bank[c % 4][:, :], bank[c % 4][:, :], rs_row[:, :], ALU.mult).then_inc(zs_v, 1)

            def heads(ap):
                return ap.rearrange("p (h d) -> p h d", d=HD)

            def dt_x(n):
                c, g = n // 2, n % 2
                dve.wait_ge(xt_t, n + 1)
                dve.tensor_tensor(heads(x_dt[:, c, g * T:(g + 1) * T]), heads(bank[6 + g][:, :]),
                                  dt_tok[:, c, g * HG:(g + 1) * HG].unsqueeze(2).to_broadcast([P, HG, HD]),
                                  ALU.mult).then_inc(xt_v, 1)

            def decay_x(n):
                c, g = n // 2, n % 2
                dve.wait_ge(xt_v, n + 1)
                if n >= 2:
                    dve.wait_ge(st_t, n - 1)
                dve.tensor_tensor(heads(x_dec[:, g, :]), heads(x_dt[:, c, g * T:(g + 1) * T]),
                                  wdec[:, c, g * HG:(g + 1) * HG].unsqueeze(2).to_broadcast([P, HG, HD]),
                                  ALU.mult).then_inc(xdec_v, 1)

            def state(n):
                c, g = n // 2, n % 2
                gs = slice(g * T, (g + 1) * T)
                dve.wait_ge(st_t, n + 1)
                if c == 0:
                    dve.tensor_copy(hst[:, 0, gs], bank[4 + g][:, :]).then_inc(st_v, 1)
                    return
                dve.wait_ge(st_v, n - 1)
                dve.tensor_tensor(heads(hst[:, c, gs]), heads(hst[:, c - 1, gs]),
                                  dend[:, c, g * HG:(g + 1) * HG].unsqueeze(2).to_broadcast([P, HG, HD]),
                                  ALU.mult).then_inc(st_m, 1)
                dve.wait_ge(st_m, n - 1)
                dve.tensor_tensor(hst[:, c, gs], hst[:, c, gs], bank[4 + g][:, :], ALU.add).then_inc(st_v, 1)

            for c in range(4):
                scale_z(c)
            conv(DK // 2 + XT // 4)
            scale_z(4)
            for g in range(GROUPS):
                dve.wait_ge(cbm_t, g + 1)
                dve.tensor_tensor(g_mask[:, g, :, :], bank[6 + g][:, :].rearrange("p (c t) -> p c t", c=SC),
                                  tri[:, :].unsqueeze(1).to_broadcast([P, SC, P]), ALU.mult).then_inc(cbm_v, 1)
            scale_z(5)
            dt_x(0)
            dt_x(1)
            scale_z(6)
            dt_x(2)
            dt_x(3)
            scale_z(7)
            dve.wait_ge(acs_s, 2)
            dve.wait_ge(w_used, 2 * IT_OUT)
            decay_x(0)
            decay_x(1)
            dt_x(4)
            dt_x(5)
            state(0)
            state(1)
            decay_x(2)
            decay_x(3)
            dt_x(6)
            dt_x(7)
            state(2)
            state(3)
            decay_x(4)
            decay_x(5)
            state(4)
            state(5)

            def finish(q):
                b = 6 + q % 2
                dve.wait_ge(diag_t, q + 1)
                dve.wait_ge(off_v, q + 1)
                dve.tensor_tensor(bank[b][:, P:], bank[b][:, P:], e_t[:, q % 2, P:], ALU.add).then_inc(y_a, 1)
                dve.wait_ge(y_a, q + 1)
                dve.scalar_tensor_tensor(out=bank[b][:, :], in0=xbc[:, q, :], scalar=d_col[:, q:q + 1],
                                         in1=bank[b][:, :], op0=ALU.mult, op1=ALU.add).then_inc(y_d, 1)
                dve.wait_ge(y_d, q + 1)
                dve.wait_ge(z_done, q + 1)
                dve.tensor_tensor(z[:, q, :], z[:, q, :], bank[b][:, :], ALU.mult).then_inc(y_v, 1)

            def norm_y(g):
                dve.wait_ge(ssdn[g].row, 1)
                for k in range(DK // GROUPS * g, DK // GROUPS * (g + 1)):
                    dve.scalar_tensor_tensor(out=z[:, k, :], in0=z[:, k, :], scalar=col("ssd_norm_g", k),
                                             in1=bank[4 + g][:, :], op0=ALU.mult, op1=ALU.mult).then_inc(ssdn[g].val, 1)

            def rest_y(g, k):
                m = DK // GROUPS * g + k
                dve.wait_ge(ssdn[g].hi, k + 1)
                dve.tensor_tensor(ysl[:, m, :], z[:, m, :], ysh[:, m, :].bitcast(F32), ALU.subtract).then_inc(ssdn[g].lo, 1)

            for q in range(DK):
                g = q // (DK // GROUPS)
                for e in range(2):
                    h = 2 * q + e
                    dve.wait_ge(l_s, h + 1)
                    if q >= 2:
                        dve.wait_ge(diag_t, q - 1)
                    dve.tensor_tensor(m_t[:, h % 4, :], l_t[:, e, :], g_mask[:, g, :, :].rearrange("p c t -> p (c t)"),
                                      ALU.mult).then_inc(m_v, 1)
                dve.wait_ge(e_s, q + 1)
                dve.wait_ge(off_t, q + 1)
                dve.tensor_tensor(e_t[:, q % 2, P:], e_t[:, q % 2, P:], bank[4 + q % 2][:, P:], ALU.mult).then_inc(off_v, 1)
                if q:
                    finish(q - 1)
                if q == DK // 2 + 2:
                    invert(ssdn[0])
                if q == DK - 1:
                    norm_y(0)
            finish(DK - 1)
            for k in range(DK // GROUPS):
                rest_y(0, k)
            invert(ssdn[1])
            norm_y(1)
            dve.wait_ge(mu_row, 1)
            for c in range(DK):
                if c % 2:
                    rest_y(1, c // 2)
                dve.tensor_tensor(u[:, c, :], u[:, c, :], bank[6][:, :], ALU.add).then_inc(cen_v, 1)
            invert(lnn)
            dve.wait_ge(lnn.row, 1)
            for c in range(DK):
                dve.scalar_tensor_tensor(out=u[:, c, :], in0=u[:, c, :], scalar=col("conf_ln_g", c), in1=bank[7][:, :],
                                         op0=ALU.mult, op1=ALU.mult).then_inc(lnn.val, 1)
            for c in range(DK):
                dve.wait_ge(lnn.hi, c + 1)
                dve.tensor_tensor(ycl[:, c, :], u[:, c, :], ych[:, c, :].bitcast(F32), ALU.subtract).then_inc(lnn.lo, 1)

            clear(postm)
            for m in range(DK):
                add_square(postm, m, out_bank(m))
            post_norm(postm, "mix_post_g", lambda k: rest_x(pre2, "ffn2_pre_g", k))
            invert(pre2)
            keep_row(pre2)
            gate_up(1, IT_GU2, PR_GU2)
            dve.wait_ge(w_used, 2 * IT_DOWN2)
            clear(post2)
            add_down(post2)
            post_norm(post2, "ffn2_post_g", lambda k: None)
            for c in range(SC):
                dve.wait_ge(out_turned, SC + c + 1)
                dve.tensor_copy(x_tok[:, c, T:2 * T], bank[4 + c][:, :]).then_inc(out_copied[1], 1)

        @block.tensor
        def _(pe):
            def three(dst, s, blk, t, hi, lo, first, last):
                c0 = blk * CW + t * P
                pe.matmul(dst, w_lo[s][:, c0:c0 + P], hi, start=first, stop=False)
                pe.matmul(dst, w_hi[s][:, c0:c0 + P], lo, start=False, stop=False)
                return pe.matmul(dst, w_hi[s][:, c0:c0 + P], hi, start=False, stop=last)

            def project(it, free, after=None):
                for s in range(2):
                    pe.wait_ge(lo_done, it * 2 + (s + 1))
                    for t in range(2):
                        for sm, v in free(2 * s + t):
                            pe.wait_ge(sm, v)
                        for k in range(DK):
                            last = three(bank[2 * s + t][:, :], s, k, t, xh[:, k, :], xl[:, k, :], k == 0, k == DK - 1)
                        last.then_inc(w_used if t else tile_done[s], 1)
                        if after:
                            after(2 * s + t)

            def sums(nm, src, b, first, last):
                for c in range(SC):
                    mm = pe.matmul(bank[b][:, c:c + 1], src[:, c * P:(c + 1) * P], ones[:, 0:1],
                                   start=(first and c == 0), stop=(last and c == SC - 1), skip_group_check=True)
                if nm:
                    mm.then_inc(nm.sum, 1)
                return mm

            def spread(src, b, done):
                for c in range(SC):
                    mm = pe.matmul(bank[b][:, c * P:(c + 1) * P], src[:, c:c + 1].to_broadcast([P, P]), ident[:, :],
                                   start=True, stop=True)
                mm.then_inc(done, 1)

            def first_project(nm, it, before=None):
                half = DK // 2

                def blocks(b, ks):
                    for k in ks:
                        last = three(bank[b][:, :], b // 2, k, b % 2, xh[:, k, :], xl[:, k, :], k == 0, k == DK - 1)
                    if ks[-1] == DK - 1:
                        last.then_inc(w_used if b % 2 else tile_done[b // 2], 1)
                for k in range(half):
                    if before:
                        before(k)
                    pe.wait_ge(nm.sq, k + 1)
                    sums(nm, sqx[k % 2], 7, k == 0, False)
                    if k == 0:
                        for s in range(2):
                            pe.wait_ge(lo_done, it * 2 + (s + 1))
                    pe.wait_ge(nm.lo, k + 1)
                    for b in range(4):
                        blocks(b, [k])
                for k in range(half, DK):
                    if before:
                        before(k)
                    pe.wait_ge(nm.sq, k + 1)
                    sums(nm, sqx[k % 2], 7, False, k == DK - 1)
                    pe.wait_ge(nm.lo, k + 1)
                    for b in range(2):
                        blocks(b, [k])
                blocks(2, list(range(half, DK)))
                pe.wait_ge(nm.inv, 1)
                spread(rinv, 7, nm.row)
                blocks(3, list(range(half, DK)))

            def gate_up(n, nm, it0, before=None):
                first_project(nm, it0, before)

                def free(i):
                    tl = i * 2 + (n * FK - 1)
                    return lambda b: [(silu_done if b < 2 else hl_done, tl + b % 2)]
                with pe.Fori(1, FK // 2) as i:
                    project(i + it0, free(i))

            def down(n, nm, it0):
                def pair(i, first):
                    for s in range(2):
                        if first:
                            for sm in (hh_done, hl_done):
                                pe.wait_ge(sm, n * FK + (s * KH + KH + 1) // 2 * 2)
                        pe.wait_ge(lo_done, i * 2 + (2 * it0 + s + 1))
                        for t in range(2):
                            if s == 0 and not first:
                                pe.wait_ge(nm.add, i * 2 + t)
                            for k in range(KH):
                                kk = s * KH + k
                                last = three(bank[4 + t][:, :], s, k, t, hh[:, kk, :], hl[:, kk, :], kk == 0, kk == FK - 1)
                            if t:
                                last.then_inc(w_used, 1)
                            elif s:
                                last.then_inc(acc_done, 1)
                pair(0, True)
                with pe.Fori(1, DK // 2) as i:
                    pair(i, False)

            def post_norm(nm):
                pe.wait_ge(nm.add, DK + 1)
                sums(nm, sq_norm, 6, True, True)
                pe.wait_ge(nm.inv, 1)
                spread(rinv, 6, nm.row)

            pe.wait_ge(consts, 4)
            pe.wait_ge(par_in, 16 * (len(VECS) + 3))
            at_col = 0
            for i, rows in enumerate((NVEC, STAPS * XT, HALF_ROWS, HALF_ROWS)):
                last = pe.transpose(bank[7][:, at_col:at_col + rows], par_rows[0:rows, i, :], ident[0:rows, 0:rows])
                at_col += rows
            last.then_inc(par_t, 1)
            for c in range(SC):
                pe.wait_ge(x_in[c], 16)

            def turn(k):
                if k >= 3:
                    pe.wait_ge(x_ready, k - 2)
                for c in range(SC):
                    mm = pe.transpose(bank[turn_bank(k)][:, c * P:(c + 1) * P], x_tok[:, c, k * P:(k + 1) * P], ident[:, :])
                mm.then_inc(x_turned, 1)

            for k in range(3):
                turn(k)

            def turn_next(k):
                if k == 0:
                    pe.wait_ge(par_ok, 2)
                if k + 3 < DK:
                    turn(k + 3)
            gate_up(0, pre1, IT_GU1, turn_next)
            down(0, post1, IT_DOWN1)
            post_norm(post1)
            first_project(prem, IT_GLU)

            pe.wait_ge(dtw_lo, 1)
            for c in range(SC):
                cs = slice(c * P, (c + 1) * P)
                for k in range(DK):
                    dst = bank[6][:, c * HEADS:(c + 1) * HEADS]
                    pe.matmul(dst, xl[:, k, cs], dtwh[:, k, :], start=(k == 0), stop=False)
                    pe.matmul(dst, xh[:, k, cs], dtwl[:, k, :], start=False, stop=False)
                    last = pe.matmul(dst, xh[:, k, cs], dtwh[:, k, :], start=False, stop=(k == DK - 1))
            last.then_inc(dt_raw, 1)

            def glu_free(i):
                return lambda b: [(ga_v, 2 * i + b + 1) if b < 2 else (u_done, 2 * i + b - 1)]
            for i in range(1, DK // 2):
                project(IT_GLU + i, glu_free(i - 1))

            def sum_decays(b):
                if b == 1:
                    pe.wait_ge(dt_v, SC + 2)
                    da = da_tok[:, :, :].rearrange("p c h -> p (c h)")
                    pe.matmul(bank[6][:, 0:64], tri[:, :], da, start=True, stop=True)
                    pe.matmul(bank[6][:, 64:128], ones[:, :], da, start=True, stop=True).then_inc(acs_t, 1)
            project(IT_XBC, glu_free(DK // 2 - 1), sum_decays)
            for i in range(1, XT // 4):
                project(IT_XBC + i, lambda b: [(cb_step, short_steps(4 * (i - 1) + b))])
            project(IT_Z, lambda b: [(cb_step, short_steps(XT - 4 + b))])
            pe.wait_ge(xbc_done, XT)
            pe.wait_ge(acs_v, 2)
            pe.wait_ge(acs_s, 2)
            for g in range(GROUPS):
                for c in range(SC):
                    last = pe.transpose(bank[6 + g][:, c * P:(c + 1) * P], xbc[:, DK + g, c * P:(c + 1) * P], ident[:, :])
                last.then_inc(bt_t, 1)

            def turn_x(n):
                c, g = n // 2, n % 2
                if n >= 2:
                    pe.wait_ge(xt_v, n - 1)
                else:
                    pe.wait_ge(cbm_v, n + 1)
                for j in range(4):
                    last = pe.transpose(bank[6 + g][:, j * P:(j + 1) * P], xbc[:, 4 * g + j, c * P:(c + 1) * P], ident[:, :])
                last.then_inc(xt_t, 1)

            def between(b):
                if b == 0:
                    for g in range(GROUPS):
                        pe.wait_ge(bt_c, g + 1)
                        for c in range(SC):
                            cs = slice(c * P, (c + 1) * P)
                            last = pe.matmul(bank[6 + g][:, cs], xbc[:, DK + g, cs], xbc[:, DK + GROUPS + g, cs],
                                             start=True, stop=True)
                        last.then_inc(cbm_t, 1)
                else:
                    turn_x(2 * b - 2)
                    turn_x(2 * b - 1)
            project(IT_Z + 1, lambda b: [(z_done, b + 1)], between)

            def state(n):
                c, g = n // 2, n % 2
                pe.wait_ge(xdec_v, n + 1)
                if n >= 2:
                    pe.wait_ge(st_v, n - 1)
                else:
                    pe.wait_ge(cv_out, 3 + n)
                pe.matmul(bank[4 + g][:, :], b_tok[:, g, c, :], x_dec[:, g, :], start=True, stop=True).then_inc(st_t, 1)

            def decays(q):
                if q:
                    pe.wait_ge(seg_s, 2 * SC * q)
                    pe.wait_ge(e_s, q)
                else:
                    pe.wait_ge(z_done, 7)
                    pe.wait_ge(da_s, 2)
                    pe.wait_ge(da_v, 1)
                for c in range(SC):
                    cs = slice(c * P, (c + 1) * P)
                    for e in range(2):
                        h = c * HEADS + 2 * q + e
                        pe.matmul(bank[e][:, cs], da_hi[:, h:h + 1].to_broadcast([P, P]), tri_r[:, :], start=True, stop=False)
                        pe.matmul(bank[e][:, cs], da_lo[:, h:h + 1].to_broadcast([P, P]), tri_r[:, :], start=False, stop=True)
                    for e in range(2):
                        last = pe.matmul(bank[2][e * HD:(e + 1) * HD, cs],
                                         da_tok[:, c, 2 * q + e:2 * q + e + 1].to_broadcast([P, HD]), tri[:, :],
                                         start=True, stop=True)
                last.then_inc(r_t, 1)

            def off(q):
                g = q // (DK // GROUPS)
                if q >= 2:
                    pe.wait_ge(off_v, q - 1)
                for c in range(1, SC):
                    cs = slice(c * P, (c + 1) * P)
                    last = pe.matmul(bank[4 + q % 2][:, cs], hst[:, c - 1, q * P:(q + 1) * P], xbc[:, DK + GROUPS + g, cs],
                                     start=True, stop=True)
                last.then_inc(off_t, 1)

            def diag(q):
                if q >= 2:
                    pe.wait_ge(y_v, q - 1)
                for e in range(2):
                    h = 2 * q + e
                    pe.wait_ge(m_v, h + 1)
                    for c in range(SC):
                        cs = slice(c * P, (c + 1) * P)
                        last = pe.matmul(bank[6 + q % 2][e * HD:(e + 1) * HD, cs], x_dt[:, c, h * HD:(h + 1) * HD],
                                         m_t[:, h % 4, cs], start=True, stop=True)
                last.then_inc(diag_t, 1)

            def sum_y(q):
                g, k = q // (DK // GROUPS), q % (DK // GROUPS)
                if k == 0:
                    if g:
                        pe.wait_ge(ssdn[0].root, 1)
                    else:
                        pe.wait_ge(z_done, DK)
                pe.wait_ge(ssdn[g].sq, k + 1)
                sums(ssdn[g], sq_y[q % 2], 3, k == 0, k == DK // GROUPS - 1)

            state(0)
            state(1)
            decays(0)
            turn_x(6)
            turn_x(7)
            for n in range(2, 6):
                state(n)
            pe.wait_ge(st_v, 6)
            pe.wait_ge(xt_v, 2 * SC)
            for q in range(DK):
                off(q)
                if q + 1 < DK:
                    decays(q + 1)
                else:
                    pe.wait_ge(ssdn[0].inv, 1)
                    pe.wait_ge(off_v, DK - 1)
                    spread(rinv, 4, ssdn[0].row)
                diag(q)
                if q:
                    sum_y(q - 1)
            sum_y(DK - 1)
            order = list(range(2 * POOL_PAIRS, DK)) + list(range(2 * POOL_PAIRS))
            pe.wait_ge(cv_out, DK - 2 * POOL_PAIRS)
            pe.wait_ge(y_v, DK - 1)
            for n, c in enumerate(order):
                if c < 2 * POOL_PAIRS:
                    pe.wait_ge(cp_out, c + 1)
                last = sums(None, u[:, c, :], 6, n == 0, n == DK - 1)
            last.then_inc(mu_t, 1)
            pe.wait_ge(ssdn[1].inv, 1)
            pe.wait_ge(off_v, DK)
            spread(rinv, 5, ssdn[1].row)
            pe.wait_ge(mu_s, 1)
            spread(rms, 6, mu_row)

            def out_tile(j, t):
                half, m = OUT_CHUNKS[j]
                hi, lo = (ych, ycl) if half else (ysh, ysl)
                b = out_bank(2 * m + t)
                if t == 0:
                    pe.wait_ge(lo_done, 2 * IT_OUT + j + 1)
                if half == 0 and 2 * m + t >= 6:
                    pe.wait_ge(postm.add, 2 * m + t - 6 + 2)
                for k in range(DK):
                    if j == 0 and t == 0:
                        pe.wait_ge(ssdn[k // (DK // GROUPS)].lo, k % (DK // GROUPS) + 1)
                    if j == OUT_CHUNKS.index((1, 0)) and t == 0:
                        pe.wait_ge(lnn.lo, k + 1)
                    last = three(bank[b][:, :], j % 2, k, t, hi[:, k, :], lo[:, k, :], half == 0 and k == 0,
                                 half == 1 and k == DK - 1)
                if t:
                    last.then_inc(w_used, 1)
                elif half:
                    last.then_inc(acc_done, 1)

            for j in range(len(OUT_CHUNKS)):
                out_tile(j, 0)
                if j == 1:
                    pe.wait_ge(lnn.inv, 1)
                    spread(rinv, 7, lnn.row)
                out_tile(j, 1)
                if j == 0:
                    for c in range(DK):
                        pe.wait_ge(lnn.sq, c + 1)
                        sums(lnn, sq_y[c % 2], 7, c == 0, c == DK - 1)
            post_norm(postm)
            gate_up(1, pre2, IT_GU2)
            down(1, post2, IT_DOWN2)
            post_norm(post2)
            for h in range(2):
                pe.wait_ge(post2.val, DK // 2 * (h + 1))
                for c in range(SC):
                    for j in range(4):
                        last = pe.transpose(bank[4 * h + c][:, j * P:(j + 1) * P], x[:, 4 * h + j, c * P:(c + 1) * P], ident[:, :])
                    last.then_inc(out_turned, 1)


def short_steps(c):
    return (c // 2) * 2 * (STAPS - 1) + 2 * (STAPS - 2) + c % 2 + 1


_INS = ["x", "ffn1_pre_g", "ffn1_w_gate", "ffn1_w_up", "ffn1_w_down", "ffn1_post_g", "mix_pre_g", "w_in", "b_glu",
        "ssd_conv_w", "ssd_conv_b", "dt_bias", "a_log", "d_skip", "ssd_norm_g", "conf_dw_w", "conf_dw_b",
        "conf_ln_g", "conf_ln_b", "w_out", "mix_post_g", "ffn2_pre_g", "ffn2_w_gate", "ffn2_w_up", "ffn2_w_down",
        "ffn2_post_g"]


def kernel(**inputs):
    import numpy as _np
    import concourse.bacc as _bacc
    from concourse import mybir as _mybir
    from concourse.bass_utils import run_bass_kernel_spmd as _run

    nc = _bacc.Bacc("TRN2", target_bir_lowering=False, num_devices=1)
    arrays, args = {}, {}
    for name in _INS:
        arr = _np.ascontiguousarray(inputs[name])
        arrays[f"in_{name}"] = arr
        args[name] = nc.dram_tensor(f"in_{name}", arr.shape, _mybir.dt.from_np(arr.dtype), kind="ExternalInput").ap()
    out = nc.dram_tensor("out_x", (1, T, D), F32, kind="ExternalOutput").ap()
    build(nc, args, out)
    r = _run(nc, [arrays], core_ids=[0])
    return r.results[0]["out_x"]
```

```python
from contextlib import ExitStack

import concourse.bass as bass
from concourse import mybir

ALU = mybir.AluOpType
ACT = mybir.ActivationFunctionType
F32 = mybir.dt.float32
F32R = mybir.dt.float32r

P = 128
T = 512
D = 1024
FF = 2816
DK = D // P
FK = FF // P
KH = FK // 2
CW = 256
D_SSM = 1024
STATE = 128
GROUPS = 2
HEADS = 16
HD = 64
XBC = D_SSM + 2 * GROUPS * STATE
XT = XBC // P
D_CONV = 1024
TAPS = 31
STAPS = 4
SC = T // P
HG = HEADS // GROUPS
EPS = 1e-6

Z0 = 0
XBC0 = D_SSM
DT0 = XBC0 + XBC
GLU0 = DT0 + HEADS

IT_GU1 = 0
IT_DOWN1 = IT_GU1 + FK // 2
IT_GLU = IT_DOWN1 + DK // 2
IT_XBC = IT_GLU + DK // 2
IT_Z = IT_XBC + XT // 4
IT_OUT = IT_Z + DK // 4
IT_GU2 = IT_OUT + DK // 2
IT_DOWN2 = IT_GU2 + FK // 2
IT_END = IT_DOWN2 + DK // 2
PR_GU1 = 0
PR_GLU = FK // 2
PR_XBC = PR_GLU + DK // 2
PR_Z = PR_XBC + XT // 4
PR_GU2 = PR_Z + DK // 4
AC_DOWN1 = 0
AC_OUT = DK // 2
AC_DOWN2 = DK

VECS = [("ffn1_pre_g", 8), ("ffn1_post_g", 8), ("mix_pre_g", 8), ("mix_post_g", 8), ("ffn2_pre_g", 8),
        ("ffn2_post_g", 8), ("ssd_norm_g", 8), ("conf_ln_g", 8), ("conf_ln_b", 8), ("conf_dw_b", 8),
        ("b_glu", 16), ("ssd_conv_b", 12)]
COL = {}
_at = 0
for _n, _k in VECS:
    COL[_n] = _at
    _at += _k
NVEC = _at
COL["ssd_conv_w"] = NVEC
COL["conf_dw_w"] = NVEC + STAPS * XT
HALF_ROWS = TAPS * DK // 2
NPAR = NVEC + STAPS * XT + TAPS * DK


STEPS = TAPS - 1
SHARED = 22
DVE_JOBS = [(0, 1, STEPS), (2, 1, STEPS), (3, 1, SHARED)]
POOL_JOBS = [(1, 1, STEPS), (3, SHARED + 1, STEPS)]


def steps_of(jobs):
    return [(j, pair, back, back == first, back == last) for j, (pair, first, last) in enumerate(jobs)
            for back in range(first, last + 1)]


DVE_STEPS, POOL_STEPS = steps_of(DVE_JOBS), steps_of(POOL_JOBS)


def pool_turns(n):
    return [(e, 2 * n + e) for e in range(2)] if n < STEPS else [(0, STEPS + n)]
DVE_PLAN = ([0] * 4 + [3, 3, 3, 4] * 2 + [4, 3, 3, 2] + [3, 1, 3, 1] * 2 + [3, 1, 2, 2] +
            [3, 3, 3, 3] + [3, 3, 2, 0])
POOL_PLAN = [0, 0, 4, 4, 4, 4, 4, 4, 6] + [STEPS - SHARED]


def starts(plan):
    return [sum(plan[:n]) for n in range(len(plan) + 1)]


DVE_AT, POOL_AT = starts(DVE_PLAN), starts(POOL_PLAN)
assert DVE_AT[-1] == len(DVE_STEPS) and POOL_AT[-1] == len(POOL_STEPS)
assert all(n in DVE_AT for n, step in enumerate(DVE_STEPS) if step[3])

OUT_CHUNKS = [(0, 0), (0, 1), (0, 2), (1, 0), (1, 1), (1, 2), (0, 3), (1, 3)]


def out_bank(m):
    return m if m < 6 else m - 6


def end_bank(h, c):
    return (4, 5, 7, 0)[c] if h else c


def turn_bank(k):
    return 4 + k % 3


def build(nc, a, out):
    ctx = ExitStack()
    with ctx:
        def sem(name):
            return ctx.enter_context(nc.semaphore(name))

        top = [(nc.sbuf_base + 63) // 64 * 64]

        def region(size):
            at = top[0]
            top[0] += (size + 31) // 32 * 32
            assert top[0] <= nc.sbuf_usable_end, (top[0], nc.sbuf_usable_end)
            return at

        def at(name, shape, dt, offset):
            return nc.alloc_sbuf_tensor_at(name, shape, dt, offset=offset)

        WB = KH * CW * 4
        TB = T * 4
        raw_at = [region(WB) for _ in range(2)]
        w_raw = [at(f"w_raw{s}", [P, KH * CW], F32, raw_at[s]) for s in range(2)]
        hi_at = [region(WB) for _ in range(2)]
        lo_at = [region(WB) for _ in range(2)]
        w_hi = [at(f"w_hi{s}", [P, KH * CW], F32R, hi_at[s]) for s in range(2)]
        w_lo = [at(f"w_lo{s}", [P, KH * CW], F32R, lo_at[s]) for s in range(2)]

        X_AT, XH_AT, XL_AT = region(DK * TB), region(DK * TB), region(DK * TB)
        x = at("x_res", [P, DK, T], F32, X_AT)
        xh = at("xh", [P, DK, T], F32R, XH_AT)
        xl = at("xl", [P, DK, T], F32R, XL_AT)
        fo = at("fo", [P, DK, T], F32, XH_AT)
        sq_norm = at("sq_norm", [P, T], F32, XL_AT)
        sq_out = at("sq_out", [P, T], F32, XL_AT + TB)

        HB = region(2 * FK * TB)

        tails = [b + DK * CW * 4 for b in (raw_at[0], raw_at[1], hi_at[0], hi_at[1], lo_at[0], lo_at[1])]
        rs_row = at("rs_row", [P, T], F32, tails[5])
        sqx = [at(f"sqx{i}", [P, T], F32, tails[1 + i]) for i in range(2)]
        sq_sum = at("sq_sum", [P, T], F32, tails[3])
        cv_sum = [at(f"cv_sum{e}", [P, T], F32, tails[e]) for e in (1, 2)]
        cv_prod = [at(f"cv_prod{i}", [P, T], F32, tails[n]) for i, n in enumerate((3, 4, 0))]

        def slot(name, s, shape, dt):
            return at(name, shape, dt, HB + s * TB)

        hh = slot("hh", 0, [P, FK, T], F32R)
        hl = slot("hl", FK, [P, FK, T], F32R)
        hs = slot("hs", FK, [P, FK, T], F32)
        x_tok = slot("x_tok", 0, [P, SC, D], F32)
        par_rows = slot("par_rows", 8, [P, 4, P], F32)
        u = slot("u", 0, [P, DK, T], F32)
        xbc = slot("xbc", 8, [P, XT, T], F32)
        z = slot("z", 20, [P, DK, T], F32)
        x_dt = slot("x_dt", 28, [P, SC, D_SSM], F32)
        b_tok = slot("b_tok", 36, [P, GROUPS, SC, STATE], F32)
        g_mask = slot("g_mask", 38, [P, GROUPS, SC, P], F32)
        dtw = slot("dtw", 42, [P, DK, HEADS], F32)
        dtwh = at("dtwh", [P, DK, HEADS], F32R, HB + 42 * TB + 512)
        dtwl = at("dtwl", [P, DK, HEADS], F32R, HB + 42 * TB + 1024)
        acs_hi = slot("acs_hi", 43, [HEADS, T], F32R)
        acs_lo = slot("acs_lo", 40, [HEADS, T], F32R)
        pick_two = at("pick_two", [HEADS, HEADS, HD], F32R, XH_AT + 6 * TB)
        sq_y = [slot(f"sq_y{i}", 41 + i, [P, T], F32) for i in range(2)]
        dt_row = slot("dt_row", 41, [HEADS, T], F32)
        x_dec = slot("x_dec", 41, [P, 2, T], F32)
        hst = at("hst", [P, SC - 1, D_SSM], F32, XH_AT)
        l_t = at("l_t", [P, 2, T], F32, XL_AT)
        e_t = at("e_t", [P, 2, T], F32, XL_AT + 2 * TB)
        m_t = at("m_t", [P, 4, T], F32, XL_AT + 4 * TB)
        ysh = slot("ysh", 8, [P, DK, T], F32R)
        ysl = slot("ysl", 20, [P, DK, T], F32R)
        ych = slot("ych", 28, [P, DK, T], F32R)
        ycl = slot("ycl", 0, [P, DK, T], F32R)

        def small(name, shape):
            n = 4
            for d in shape[1:]:
                n *= d
            return at(name, shape, F32, region(n))

        par = small("par", [P, NPAR])
        ones = small("ones", [P, P])
        tri = small("tri", [P, P])
        ident = small("ident", [P, P])
        less_mean = small("less_mean", [P, P])
        pick_one = at("pick_one", [HEADS, HEADS], F32R, region(HEADS * 4))
        d_col = small("d_col", [P, DK])
        eps = small("eps", [P, 1])
        spare = small("spare", [P, 2])
        dtb = small("dtb", [P, HEADS])
        alog = small("alog", [P, HEADS])
        dt_tok = small("dt_tok", [P, SC, HEADS])
        da_tok = small("da_tok", [P, SC, HEADS])
        t_abs = small("t_abs", [P, SC, HEADS])
        acs = small("acs", [P, SC, HEADS])
        dend = small("dend", [P, SC, HEADS])
        wdec = small("wdec", [P, SC, HEADS])

        rms = small("rms", [P, SC])
        rinv = small("rinv", [P, SC])
        bank = [nc.alloc_psum_tensor(f"bank{b}", [P, T], F32) for b in range(8)]

        def col(name, k):
            c = COL[name] + k
            return par[:, c:c + 1]

        raw_in = [sem(f"raw_in{s}") for s in range(2)]
        hi_done = sem("hi_done")
        lo_done = sem("lo_done")
        w_used = sem("w_used")
        x_in = sem("x_in")
        par_in = sem("par_in")
        small_in = sem("small_in")
        consts_cleared = sem("consts_cleared")
        consts = sem("consts")
        par_t = sem("par_t")
        par_ok = sem("par_ok")
        x_turned = sem("x_turned")
        x_ready = sem("x_ready")
        tile_done = [sem(f"tile_done{s}") for s in range(2)]
        acc_done = sem("acc_done")
        gate_v = sem("gate_v")
        silu_done = sem("silu_done")
        up_v = sem("up_v")
        hh_done = sem("hh_done")
        hl_done = sem("hl_done")
        fo_done = sem("fo_done")
        out_turned = sem("out_turned")
        out_copied = [sem(f"out_copied{h}") for h in range(2)]
        stored = sem("stored")

        class Norm:

            def __init__(self, n, pre=False, post=False, split=False, mean=False):
                self.sq = sem(f"{n}_sq")
                self.sum = sem(f"{n}_sum")
                self.root = sem(f"{n}_root")
                self.inv = sem(f"{n}_inv")
                self.row = sem(f"{n}_row")
                if pre or split:
                    self.hi = sem(f"{n}_hi")
                    self.lo = sem(f"{n}_lo")
                if pre:
                    self.rs = sem(f"{n}_rs")
                if post or split:
                    self.val = sem(f"{n}_val")
                if pre or post or mean:
                    self.add = sem(f"{n}_add")
                if post:
                    self.a = sem(f"{n}_a")

        pre1, prem, pre2 = (Norm(n, pre=True) for n in ("pre1", "prem", "pre2"))
        post1, postm, post2 = (Norm(n, post=True) for n in ("post1", "postm", "post2"))
        ssdn = [Norm(f"ssdn{g}", split=True, mean=True) for g in range(GROUPS)]
        lnn = Norm("lnn", split=True, mean=True)
        val_pool = sem("val_pool")

        dtw_hi = sem("dtw_hi")
        dtw_lo = sem("dtw_lo")
        dt_t = sem("dt_t")
        dt_scaled = sem("dt_scaled")
        dt_v = sem("dt_v")
        dt_s = sem("dt_s")
        acs_t = sem("acs_t")
        acs_v = sem("acs_v")
        acs_s = sem("acs_s")
        ga_v = sem("ga_v")
        gg_v = sem("gg_v")
        sg_done = sem("sg_done")
        u_done = sem("u_done")
        cv_start = sem("cv_start")
        cv_step = sem("cv_step")
        cv_out = sem("cv_out")
        cp_start = sem("cp_start")
        cp_prod = sem("cp_prod")
        cp_step = sem("cp_step")
        cp_out = sem("cp_out")
        xs_v = sem("xs_v")
        cb_start = sem("cb_start")
        cb_step = sem("cb_step")
        xbc_done = sem("xbc_done")
        zs_v = sem("zs_v")
        z_done = sem("z_done")
        bt_t = sem("bt_t")
        bt_c = sem("bt_c")
        cbm_t = sem("cbm_t")
        cbm_v = sem("cbm_v")
        xt_t = sem("xt_t")
        xt_v = sem("xt_v")
        xdec_v = sem("xdec_v")
        st_t = sem("st_t")
        st_v = sem("st_v")
        st_m = sem("st_m")
        acs_split = sem("acs_split")
        r_t = sem("r_t")
        seg_s = sem("seg_s")
        l_s = sem("l_s")
        e_s = sem("e_s")
        m_v = sem("m_v")
        off_t = sem("off_t")
        off_v = sem("off_v")
        diag_t = sem("diag_t")
        y_a = sem("y_a")
        y_d = sem("y_d")
        y_v = sem("y_v")
        mu_t = sem("mu_t")
        cen_v = sem("cen_v")
        ln_act = sem("ln_act")

        def wait_tile(eng, b, it, pr):
            if b % 2 == 0:
                eng.wait_ge(tile_done[b // 2], pr + 1)
            else:
                eng.wait_ge(w_used, it * 2 + (1 + b // 2))

        def wait_out(eng, t, it, ac):
            if t == 0:
                eng.wait_ge(acc_done, ac + 1)
            else:
                eng.wait_ge(w_used, it * 2 + 2)

        block = ctx.enter_context(nc.Block())

        @block.sync
        def _(sp):
            def load_parameters():
                row = 0
                for name, k in VECS:
                    sp.dma_start(par_rows[row:row + k, 0, :], a[name].rearrange("l (k p) -> (l k) p", p=P)).then_inc(par_in, 16)
                    row += k
                sp.dma_start(par_rows[0:STAPS * XT, 1, :],
                              a["ssd_conv_w"].rearrange("l j (t p) -> (l j t) p", p=P)).then_inc(par_in, 16)
                cw = a["conf_dw_w"].rearrange("l j (t p) -> (l j t) p", p=P)
                for h in range(2):
                    sp.dma_start(par_rows[0:HALF_ROWS, 2 + h, :], cw[h * HALF_ROWS:(h + 1) * HALF_ROWS, :]).then_inc(par_in, 16)
                sp.dma_start(dtb[:, :], a["dt_bias"].to_broadcast([P, HEADS])).then_inc(small_in, 16)
                sp.dma_start(alog[:, :], a["a_log"].to_broadcast([P, HEADS])).then_inc(small_in, 16)
                dsk = a["d_skip"].rearrange("l (t h) -> l h t", h=2)
                with nc.allow_non_contiguous_dma(reason="16 values"):
                    for h in range(2):
                        sp.dma_start(d_col[h * HD:(h + 1) * HD, :], dsk[:, h, :].to_broadcast([HD, DK])).then_inc(small_in, 16)

            def load(it, srcs, first=False, slots=(0, 1)):
                for s in slots:
                    if not first:
                        sp.wait_ge(lo_done, it * 2 + (s - 1))
                    kn = srcs[s].shape[1]
                    sp.dma_start(w_raw[s][:, 0:kn * CW].rearrange("p (k n) -> p k n", k=kn),
                                 srcs[s]).then_inc(raw_in[s], 16)

            def ffn(n, it0, first):
                wg, wu, wd = (a[f"ffn{n}_w_{m}"][0].rearrange("(k p) f -> p k f", p=P) for m in ("gate", "up", "down"))
                if first:
                    load(0, [wg[:, :, 0:CW], wu[:, :, 0:CW]], True, (0,))
                    for c in range(SC):
                        sp.dma_start(x_tok[:, c, :], a["x"][0, c * P:(c + 1) * P, :]).then_inc(x_in, 16)
                    load_parameters()
                    load(0, [wg[:, :, 0:CW], wu[:, :, 0:CW]], True, (1,))
                with sp.Fori(1 if first else 0, FK // 2) as i:
                    load(i + it0, [wg[:, :, bass.ds(i * CW, CW)], wu[:, :, bass.ds(i * CW, CW)]])
                with sp.Fori(0, DK // 2) as m:
                    load(m + (it0 + FK // 2), [wd[:, h * KH:(h + 1) * KH, bass.ds(m * CW, CW)] for h in range(2)])

            ffn(1, IT_GU1, True)
            w_in = a["w_in"][0].rearrange("(k p) f -> p k f", p=P)
            with sp.Fori(0, DK // 2) as i:
                load(i + IT_GLU, [w_in[:, :, bass.ds(i * CW + (GLU0 + j * D_CONV), CW)] for j in range(2)])
            with sp.Fori(0, XT // 4) as i:
                load(i + IT_XBC, [w_in[:, :, bass.ds(i * (2 * CW) + (XBC0 + j * CW), CW)] for j in range(2)])
            with sp.Fori(0, DK // 4) as i:
                load(i + IT_Z, [w_in[:, :, bass.ds(i * (2 * CW) + (Z0 + j * CW), CW)] for j in range(2)])
            w_out = a["w_out"][0].rearrange("(k p) f -> p k f", p=P)
            for i in range(len(OUT_CHUNKS) // 2):
                load(IT_OUT + i, [w_out[:, h * DK:(h + 1) * DK, m * CW:(m + 1) * CW] for h, m in OUT_CHUNKS[2 * i:2 * i + 2]])
            ffn(2, IT_GU2, False)
            for h in range(2):
                for c in range(SC):
                    sp.wait_ge(out_copied[h], c + 1)
                    sp.dma_start(out[0, c * P:(c + 1) * P, h * T:(h + 1) * T], x_tok[:, c, h * T:(h + 1) * T]).then_inc(stored, 16)
            sp.wait_ge(stored, 16 * 2 * SC)

        @block.gpsimd
        def _(pool):
            pool.memset(ident[:, :], 0.0).then_inc(consts_cleared, 1)
            pool.memset(tri[:, :], 1.0).then_inc(consts_cleared, 1)
            pool.memset(ones[:, :], 1.0).then_inc(consts, 1)
            pool.memset(eps[:, :], EPS).then_inc(consts, 1)
            pool.memset(less_mean[:, :], -1.0 / D_CONV).then_inc(consts, 1)
            pool.wait_ge(consts_cleared, 2)
            pool.affine_select(out=ident[:, :], in_=ident[:, :], compare_op=ALU.not_equal, fill=1.0, base=0,
                               pattern=[[-1, P]], channel_multiplier=1).then_inc(consts, 1)
            pool.affine_select(out=tri[:, :], in_=tri[:, :], compare_op=ALU.is_ge, fill=0.0, base=0,
                               pattern=[[1, P]], channel_multiplier=-1).then_inc(consts, 1)

            def rest(s, it, kn, first=False):
                pool.wait_ge(hi_done, it * 2 + (s + 1))
                if not first:
                    pool.wait_ge(w_used, it * 2 + (s - 1))
                pool.tensor_tensor(w_lo[s][:, 0:kn * CW], w_raw[s][:, 0:kn * CW], w_hi[s][:, 0:kn * CW].bitcast(F32),
                                   ALU.subtract).then_inc(lo_done, 1)

            def rests(it, kn, first=False):
                for s in range(2):
                    rest(s, it, kn, first)

            def conv(begin, end):
                for n in range(begin, end):
                    job, _, back, first, _ = POOL_STEPS[n]
                    for e, m in pool_turns(n):
                        if first:
                            pool.wait_ge(cp_start, 2 * job + e + 1)
                        else:
                            pool.wait_ge(cp_step, m - 1 if job == 0 else m)
                        pool.wait_ge(cp_prod, m + 1)
                        pool.tensor_tensor(cv_sum[e][:, back:], cv_sum[e][:, back:], cv_prod[m % 3][:, back:],
                                           ALU.add).then_inc(cp_step, 1)

            def add_squares(nm, ring, ks=range(1, DK)):
                for k in ks:
                    pool.wait_ge(nm.sq, k + 1)
                    if k > 1:
                        pool.wait_ge(nm.add, k - 1)
                    pool.tensor_tensor(sq_sum[:, :], sq_sum[:, :], ring[k % 2][:, :], ALU.add).then_inc(nm.add, 1)

            rest(0, 0, DK, True)
            add_squares(pre1, sqx, range(1, DK // 2 + 1))
            rest(1, 0, DK, True)
            add_squares(pre1, sqx, range(DK // 2 + 1, DK))
            with pool.Fori(1, IT_DOWN1) as i:
                rests(i, DK)
            def down_rests(it0, n, end):
                rest(0, it0, KH)
                pool.wait_ge(hl_done, (n + 1) * FK)
                rest(1, it0, KH)
                with pool.Fori(it0 + 1, end) as i:
                    rests(i, KH)
            down_rests(IT_DOWN1, 0, IT_GLU)
            rests(IT_GLU, DK)
            add_squares(prem, sqx)
            for n in range(IT_OUT - IT_GLU - 1):
                begin, end = POOL_AT[n], POOL_AT[n + 1]
                mid = (begin + end) // 2
                conv(begin, mid)
                rest(0, IT_GLU + n + 1, DK)
                conv(mid, end)
                rest(1, IT_GLU + n + 1, DK)
            conv(POOL_AT[-3], POOL_AT[-2])

            def add_y(q):
                g, k = q // (DK // GROUPS), q % (DK // GROUPS)
                if 0 < k < DK // GROUPS - 1:
                    pool.wait_ge(ssdn[g].sq, k + 1)
                    if k > 1:
                        pool.wait_ge(ssdn[g].add, k - 1)
                    pool.tensor_tensor(sq_y[q % 2][:, :], sq_y[q % 2][:, :], sq_y[1 - q % 2][:, :],
                                       ALU.add).then_inc(ssdn[g].add, 1)
            for q in range(DK):
                conv(POOL_AT[-2] + POOL_PLAN[-1] * q // DK, POOL_AT[-2] + POOL_PLAN[-1] * (q + 1) // DK)
                if q >= 2:
                    add_y(q - 2)
                if q == 3:
                    rest(0, IT_OUT, DK)
            add_y(DK - 2)
            add_y(DK - 1)
            rest(1, IT_OUT, DK)
            add_squares(lnn, sq_y)
            with pool.Fori(IT_OUT + 1, IT_GU2 + 1) as i:
                rests(i, DK)
            add_squares(pre2, sqx)
            with pool.Fori(IT_GU2 + 1, IT_DOWN2) as i:
                rests(i, DK)
            down_rests(IT_DOWN2, 1, IT_END)
            for k in range(1, DK - 1, 2):
                pool.wait_ge(post2.a, k + 1)
                pool.tensor_tensor(x[:, k, :], x[:, k, :], fo[:, k, :], ALU.add).then_inc(val_pool, 1)

        @block.scalar
        def _(act):
            def round_w(s, it, kn, first=False):
                act.wait_ge(raw_in[s], it * 16 + 16)
                if not first:
                    act.wait_ge(w_used, it * 2 + (s - 1))
                act.activation(w_hi[s][:, 0:kn * CW], w_raw[s][:, 0:kn * CW], ACT.Copy).then_inc(hi_done, 1)

            def table(f):
                act.activation(spare[:, 0:1], spare[:, 1:2], f)

            def root(nm, b, n, sums):
                act.wait_ge(nm.sum, sums)
                act.activation(rms[:, :], bank[b][:, 0:SC], ACT.Sqrt, bias=eps[:, 0:1], scale=1.0 / n).then_inc(nm.root, 1)

            def square(nm, k, src, ring):
                if k >= 3:
                    act.wait_ge(nm.add, k - 2)
                act.activation(ring[k % 2][:, :] if k else sq_sum[:, :], src, ACT.Square).then_inc(nm.sq, 1)

            def pre_norm(nm, gain, ready, between=lambda k: None):
                for k in range(DK):
                    between(k)
                    ready(k)
                    act.activation(xh[:, k, :], x[:, k, :], ACT.Copy, scale=col(gain, k)).then_inc(nm.hi, 1)
                    square(nm, k, x[:, k, :], sqx)
                root(nm, 7, D, 1)

            def gate_up(n, it0):
                def hidden(i, kn, first=False):
                    tl = i * 2 + n * FK
                    for t in range(2):
                        act.wait_ge(gate_v, tl + (t + 1))
                        act.activation(hs[:, i * 2 + t, :], bank[t][:, :], ACT.Silu).then_inc(silu_done, 1)
                        if t == 0 and not first:
                            round_w(0, i + (it0 + 1), kn)
                    for t in range(2):
                        if t:
                            round_w(1, i + (it0 + 1), kn)
                        act.wait_ge(up_v, 2 * tl + (2 * t + 2))
                        act.activation(hh[:, i * 2 + t, :], bank[2 + t][:, :], ACT.Copy).then_inc(hh_done, 1)
                round_w(0, it0 + 1, DK)
                table(ACT.Silu)
                hidden(0, DK, True)
                with act.Fori(1, FK // 2 - 1) as i:
                    hidden(i, DK)
                hidden(FK // 2 - 1, KH)

            def take(nm, m, b):
                act.wait_ge(nm.add, m + 1)
                act.activation(sq_out[:, :], bank[b][:, :], ACT.Square).then_inc(nm.sq, 1)
                act.activation(fo[:, m, :], bank[b][:, :], ACT.Copy).then_inc(fo_done, 1)

            def take_down(nm, it0, ac0, kn_next):
                def pair(i, kn, last=False):
                    if kn:
                        round_w(0, i + (it0 + 1), kn)
                    for t in range(2):
                        wait_out(act, t, i + it0, i + ac0)
                        take(nm, i * 2 + t, 4 + t)
                    if kn and not last:
                        round_w(1, i + (it0 + 1), kn)
                with act.Fori(0, DK // 2 - 1) as i:
                    pair(i, KH)
                table(ACT.Sqrt)
                pair(DK // 2 - 1, kn_next, True)
                root(nm, 6, D, 1)
                if kn_next:
                    round_w(1, it0 + DK // 2, kn_next)

            def square_y(q):
                g, k = q // (DK // GROUPS), q % (DK // GROUPS)
                act.wait_ge(y_v, q + 1)
                if k > 1:
                    act.wait_ge(ssdn[g].add, k - 1)
                elif g and k == 0:
                    act.wait_ge(ssdn[g - 1].sum, 1)
                act.activation(sq_y[q % 2][:, :], z[:, q, :], ACT.Square).then_inc(ssdn[g].sq, 1)

            def round_y(g):
                for k in range(DK // GROUPS):
                    act.wait_ge(ssdn[g].val, k + 1)
                    act.activation(ysh[:, 4 * g + k, :], z[:, 4 * g + k, :], ACT.Copy).then_inc(ssdn[g].hi, 1)

            round_w(0, 0, DK, True)
            act.wait_ge(consts, 5)
            act.wait_ge(par_ok, 1)
            table(ACT.Sqrt)
            act.wait_ge(par_ok, 4)
            pre_norm(pre1, "ffn1_pre_g", lambda k: act.wait_ge(x_ready, k + 1),
                     lambda k: round_w(1, 0, DK, True) if k == 2 else None)
            gate_up(0, IT_GU1)
            take_down(post1, IT_DOWN1, AC_DOWN1, DK)
            act.wait_ge(w_used, 2 * IT_GLU)
            act.wait_ge(small_in, 64)
            act.dma_start(dtw[:, :, :], a["w_in"][0].rearrange("(k p) f -> p k f", p=P)[:, :, DT0:DT0 + HEADS]).then_inc(small_in, 16)
            act.activation(pick_one[:, :], ident[0:HEADS, 0:HEADS], ACT.Copy).then_inc(acs_split, 1)
            pre_norm(prem, "mix_pre_g", lambda k: act.wait_ge(post1.val, k + 1))
            act.wait_ge(small_in, 80)
            act.activation(dtwh[:, :, :], dtw[:, :, :], ACT.Copy).then_inc(dtw_hi, 1)

            def newest_tap(dst, c, done):
                act.wait_ge(u_done, c + 1)
                act.activation(dst, u[:, c, :], ACT.Identity, bias=col("conf_dw_b", c),
                               scale=col("conf_dw_w", STEPS * DK + c)).then_inc(done, 1)

            def conv_turns(n):
                for step in range(DVE_AT[n], DVE_AT[n + 1]):
                    job, pair, _, _, last = DVE_STEPS[step]
                    if last and job < len(DVE_JOBS) - 1:
                        for e in range(2):
                            act.wait_ge(cv_step, 2 * step + 1 + e)
                            act.activation(u[:, 2 * pair + e, :], bank[4 + e][:, :], ACT.Copy).then_inc(cv_out, 1)
                if DVE_AT[n + 1] < min(DVE_AT[n + 2:n + 3] + [len(DVE_STEPS)]):
                    job, pair, _, first, _ = DVE_STEPS[DVE_AT[n + 1]]
                    if first:
                        for e in range(2):
                            if job:
                                act.wait_ge(cv_out, 2 * job - 1 + e)
                            newest_tap(bank[4 + e][:, :], 2 * pair + e, cv_start)

            def hand_over():
                for e in range(2):
                    conv_close(0, e)
                    act.wait_ge(cp_out, e + 1)
                    act.wait_ge(cv_step, 2 * len(DVE_STEPS) - 1 + e)
                    act.activation(cv_sum[e][:, :], bank[4 + e][:, :], ACT.Copy).then_inc(cp_start, 1)

            def products(begin, end):
                for n in range(begin, end):
                    _, pair, back, _, _ = POOL_STEPS[n]
                    if n == 0:
                        for e in range(2):
                            newest_tap(cv_sum[e][:, :], 2 * pair + e, cp_start)
                    for e, m in pool_turns(n):
                        c = 2 * pair + e
                        if m >= 3:
                            act.wait_ge(cp_step, m - 2)
                        act.activation(cv_prod[m % 3][:, back:], u[:, c, 0:T - back], ACT.Copy,
                                       scale=col("conf_dw_w", (STEPS - back) * DK + c)).then_inc(cp_prod, 1)

            def conv_close(job, e):
                if job == 0:
                    act.wait_ge(cp_step, 2 * STEPS - 1 + e)
                elif e == 0:
                    act.wait_ge(cp_step, STEPS + len(POOL_STEPS))
                else:
                    act.wait_ge(cv_step, 2 * len(DVE_STEPS) + STEPS - SHARED)
                act.activation(u[:, 2 * POOL_JOBS[job][0] + e, :], cv_sum[e][:, :], ACT.Copy).then_inc(cp_out, 1)

            def share(n, part, parts):
                begin, count = POOL_AT[n], POOL_PLAN[n]
                products(begin + count * part // parts, begin + count * (part + 1) // parts)

            for i in range(DK // 2):
                share(i, 0, 2)
                conv_turns(4 * i)
                round_w(0, IT_GLU + i + 1, DK)
                if i == 0:
                    table(ACT.Sigmoid)
                conv_turns(4 * i + 1)
                for t in range(2):
                    share(i, 2 + t, 4)
                    c = 2 * i + t
                    act.wait_ge(gg_v, c + 1)
                    act.activation(bank[2 + t][:, :], bank[2 + t][:, :], ACT.Sigmoid, bias=col("b_glu", DK + c)).then_inc(sg_done, 1)
                    conv_turns(4 * i + 2 + t)
                round_w(1, IT_GLU + i + 1, DK)
            act.wait_ge(dt_v, 1)
            act.activation(t_abs[:, :, :], dt_tok[:, :, :], ACT.Abs).then_inc(dt_s, 1)
            act.wait_ge(dt_s, 1)
            act.activation(t_abs[:, :, :], t_abs[:, :, :], ACT.Exp, scale=-1.0).then_inc(dt_s, 1)
            act.wait_ge(dt_s, 2)
            act.activation(t_abs[:, :, :], t_abs[:, :, :], ACT.Ln, bias=1.0).then_inc(dt_s, 1)
            act.wait_ge(small_in, 64)
            act.activation(alog[:, :], alog[:, :], ACT.Exp).then_inc(dt_s, 1)
            act.wait_ge(dt_v, 3)
            for i in range(XT // 4):
                n = DK // 2 + i

                def newest(b):
                    c = 4 * i + b
                    act.wait_ge(xs_v, c + 1)
                    act.activation(xbc[:, c, :], bank[b][:, :], ACT.Identity, bias=col("ssd_conv_b", c),
                                   scale=col("ssd_conv_w", (STAPS - 1) * XT + c)).then_inc(cb_start, 1)

                def finish(b):
                    c = 4 * i + b
                    act.wait_ge(cb_step, short_steps(c))
                    act.activation(xbc[:, c, :], xbc[:, c, :], ACT.Silu).then_inc(xbc_done, 1)
                table(ACT.Silu)
                share(n, 0, 4)
                newest(0)
                conv_turns(4 * n)
                share(n, 1, 4)
                newest(1)
                round_w(0, IT_XBC + i + 1, DK)
                finish(0)
                finish(1)
                conv_turns(4 * n + 1)
                share(n, 2, 4)
                newest(2)
                conv_turns(4 * n + 2)
                share(n, 3, 4)
                newest(3)
                round_w(1, IT_XBC + i + 1, DK)
                finish(2)
                finish(3)
                conv_turns(4 * n + 3)
                if i == 0:
                    act.wait_ge(acs_t, 2)
                    act.activation(acs_hi[:, :], bank[7][0:HEADS, :], ACT.Copy).then_inc(acs_split, 1)
            act.wait_ge(acs_v, 2)
            act.activation(wdec[:, :, :], wdec[:, :, :], ACT.Exp).then_inc(acs_s, 1)
            act.activation(dend[:, :, :].rearrange("p c h -> p (c h)"), bank[6][:, 64:128], ACT.Exp).then_inc(acs_s, 1)
            table(ACT.Silu)
            for i in range(DK // 4):
                n = DK // 2 + XT // 4 + i
                for b in range(4):
                    if b < 3:
                        share(n, b, 3)
                    act.wait_ge(zs_v, 4 * i + b + 1)
                    act.activation(z[:, 4 * i + b, :], bank[b][:, :], ACT.Silu).then_inc(z_done, 1)
                    if b == 1 or b == 3 and i == 0:
                        round_w(b // 2, IT_Z + i + 1, DK)
                    conv_turns(4 * n + b)
                    if i == 0 and b == 1:
                        for g in range(GROUPS):
                            act.wait_ge(bt_t, g + 1)
                            act.activation(b_tok[:, g, :, :].rearrange("p c n -> p (c n)"), bank[6 + g][:, :], ACT.Copy).then_inc(bt_c, 1)
                    if i == 1 and b == 2:
                        hand_over()
            last = len(POOL_PLAN) - 1
            act.wait_ge(w_used, 2 * IT_OUT)
            act.activation(pick_two[:, :, :], ident[0:HEADS, 0:HEADS].unsqueeze(2).to_broadcast([HEADS, HEADS, HD]),
                           ACT.Copy).then_inc(acs_split, 1)
            for q in range(DK):
                act.wait_ge(r_t, 2 * q + 1)
                for e in range(2):
                    h = 2 * q + e
                    if q:
                        act.wait_ge(m_v, h - 1)
                    for c in range(SC):
                        act.activation(l_t[:, e, c * P:(c + 1) * P], bank[e][:, c * P:(c + 1) * P], ACT.Relu,
                                       bias=acs[:, c, h:h + 1], scale=-1.0).then_inc(seg_s, 1)
                if q >= 2:
                    act.wait_ge(y_a, q - 1)
                act.wait_ge(r_t, 2 * q + 2)
                act.activation(e_t[:, q % 2, :], bank[2][:, :], ACT.Exp).then_inc(e_s, 1)
                for e in range(2):
                    act.wait_ge(seg_s, SC * (2 * q + e + 1))
                    act.activation(l_t[:, e, :], l_t[:, e, :], ACT.Exp, scale=-1.0).then_inc(l_s, 1)
                share(last, q, DK)
                if q >= 2:
                    square_y(q - 2)
            table(ACT.Sqrt)
            root(ssdn[0], 3, D_SSM // GROUPS, 1)
            square_y(DK - 2)
            square_y(DK - 1)
            for e in range(2):
                conv_close(1, e)
            root(ssdn[1], 3, D_SSM // GROUPS, 1)
            round_y(0)
            round_y(1)
            round_w(1, IT_OUT, DK)
            for c in range(DK):
                act.wait_ge(cen_v, c + 1)
                square(lnn, c, u[:, c, :], sq_y)
            root(lnn, 7, D_CONV, 1)
            for s in range(2):
                round_w(s, IT_OUT + 1, DK)
            table(ACT.Silu)
            for c in range(DK):
                act.wait_ge(lnn.val, c + 1)
                act.activation(u[:, c, :], u[:, c, :], ACT.Silu, bias=col("conf_ln_b", c)).then_inc(ln_act, 1)
                act.wait_ge(ln_act, c + 1)
                act.activation(ych[:, c, :], u[:, c, :], ACT.Copy).then_inc(lnn.hi, 1)

            for j, (half, m) in enumerate(OUT_CHUNKS):
                if half:
                    for t in range(2):
                        if t:
                            act.wait_ge(w_used, 2 * IT_OUT + j + 1)
                        else:
                            act.wait_ge(acc_done, AC_OUT + m + 1)
                        if j == len(OUT_CHUNKS) - 1 and t:
                            table(ACT.Sqrt)
                        take(postm, 2 * m + t, out_bank(2 * m + t))
                if j == len(OUT_CHUNKS) - 1:
                    root(postm, 6, D, 1)
                if j > 1:
                    round_w(j % 2, IT_OUT + j // 2 + 1, DK)
            pre_norm(pre2, "ffn2_pre_g", lambda k: act.wait_ge(postm.val, k + 1))
            gate_up(1, IT_GU2)
            take_down(post2, IT_DOWN2, AC_DOWN2, 0)
            for c in range(SC):
                act.wait_ge(out_turned, c + 1)
                act.activation(x_tok[:, c, 0:T], bank[c][:, :], ACT.Copy).then_inc(out_copied[0], 1)

        @block.vector
        def _(dve):
            def invert(nm):
                dve.wait_ge(nm.root, 1)
                dve.reciprocal(rinv[:, :], rms[:, :]).then_inc(nm.inv, 1)

            def keep_row(nm):
                dve.wait_ge(nm.row, 1)
                dve.tensor_copy(rs_row[:, :], bank[7][:, :]).then_inc(nm.rs, 1)
                dve.wait_ge(nm.rs, 1)

            def rest_x(nm, gain, k):
                dve.wait_ge(nm.hi, k + 1)
                dve.scalar_tensor_tensor(out=xl[:, k, :], in0=x[:, k, :], scalar=col(gain, k), in1=xh[:, k, :].bitcast(F32),
                                         op0=ALU.mult, op1=ALU.subtract).then_inc(nm.lo, 1)

            def gate_up(n, it0, pr0):
                with dve.Fori(0, FK // 2) as i:
                    tl = i * 2 + n * FK
                    for t in range(2):
                        wait_tile(dve, t, i + it0, i + pr0)
                        dve.tensor_tensor(bank[t][:, :], bank[t][:, :], rs_row[:, :], ALU.mult).then_inc(gate_v, 1)
                    for t in range(2):
                        dve.wait_ge(silu_done, tl + (t + 1))
                        wait_tile(dve, 2 + t, i + it0, i + pr0)
                        dve.tensor_tensor(bank[2 + t][:, :], hs[:, i * 2 + t, :], bank[2 + t][:, :], ALU.mult).then_inc(up_v, 1)
                        dve.wait_ge(up_v, 2 * tl + (2 * t + 1))
                        dve.tensor_tensor(bank[2 + t][:, :], bank[2 + t][:, :], rs_row[:, :], ALU.mult).then_inc(up_v, 1)
                    for t in range(2):
                        dve.wait_ge(hh_done, tl + (t + 1))
                        dve.tensor_tensor(hl[:, i * 2 + t, :], bank[2 + t][:, :], hh[:, i * 2 + t, :].bitcast(F32),
                                          ALU.subtract).then_inc(hl_done, 1)

            def clear(nm):
                dve.memset(sq_norm[:, :], 0.0).then_inc(nm.add, 1)

            def add_squares(nm):
                clear(nm)
                with dve.Fori(0, DK - 1) as m:
                    dve.wait_ge(nm.sq, m + 1)
                    dve.wait_ge(nm.add, m + 1)
                    dve.tensor_tensor(sq_norm[:, :], sq_norm[:, :], sq_out[:, :], ALU.add).then_inc(nm.add, 1)

            def post_norm(nm, gain, after):
                scale_out(nm, gain, 0)
                for k in range(DK):
                    add_out(nm, k)
                    if k + 1 < DK:
                        scale_out(nm, gain, k + 1)
                    after(k)

            def scale_out(nm, gain, k):
                if k == 0:
                    invert(nm)
                    dve.wait_ge(nm.row, 1)
                dve.scalar_tensor_tensor(out=fo[:, k, :], in0=fo[:, k, :], scalar=col(gain, k), in1=bank[6][:, :],
                                         op0=ALU.mult, op1=ALU.mult).then_inc(nm.a, 1)

            def add_out(nm, k):
                dve.wait_ge(nm.a, k + 1)
                dve.tensor_tensor(x[:, k, :], x[:, k, :], fo[:, k, :], ALU.add).then_inc(nm.val, 1)

            dve.memset(spare[:, :], 0.0).then_inc(par_ok, 1)
            dve.wait_ge(par_t, 1)
            dve.tensor_copy(par[:, :], bank[7][:, 0:NPAR]).then_inc(par_ok, 1)
            dve.wait_ge(par_ok, 2)
            for name in ("ffn1_post_g", "ffn2_post_g"):
                g = par[:, COL[name]:COL[name] + DK]
                dve.tensor_scalar(g, g, 0.5, None, ALU.mult).then_inc(par_ok, 1)
            dve.wait_ge(par_ok, 4)
            for k in range(DK + 2):
                if k < DK:
                    dve.wait_ge(x_turned, k + 1)
                    dve.tensor_copy(x[:, k, :], bank[turn_bank(k)][:, :]).then_inc(x_ready, 1)
                if k >= 2:
                    rest_x(pre1, "ffn1_pre_g", k - 2)
            invert(pre1)
            keep_row(pre1)
            gate_up(0, IT_GU1, PR_GU1)
            dve.wait_ge(w_used, 2 * IT_DOWN1)
            add_squares(post1)
            post_norm(post1, "ffn1_post_g", lambda k: rest_x(prem, "mix_pre_g", k))
            invert(prem)
            dve.wait_ge(dtw_hi, 1)
            dve.tensor_tensor(dtwl[:, :, :], dtw[:, :, :], dtwh[:, :, :].bitcast(F32), ALU.subtract).then_inc(dtw_lo, 1)
            keep_row(prem)

            def conv(n):
                for step in range(DVE_AT[n], DVE_AT[n + 1]):
                    job, pair, back, first, _ = DVE_STEPS[step]
                    for e in range(2):
                        c = 2 * pair + e
                        if first:
                            dve.wait_ge(cv_start, 2 * job + e + 1)
                        else:
                            dve.wait_ge(cv_step, 2 * step + e - 1)
                        dve.scalar_tensor_tensor(out=bank[4 + e][:, back:], in0=u[:, c, 0:T - back],
                                                 scalar=col("conf_dw_w", (STEPS - back) * DK + c),
                                                 in1=bank[4 + e][:, back:], op0=ALU.mult, op1=ALU.add).then_inc(cv_step, 1)

            def conv_rest(q):
                for n in range((STEPS - SHARED) * q // DK, (STEPS - SHARED) * (q + 1) // DK):
                    back, c = SHARED + 1 + n, 2 * DVE_JOBS[-1][0] + 1
                    if n == 0:
                        dve.wait_ge(cp_start, 4)
                    else:
                        dve.wait_ge(cv_step, 2 * len(DVE_STEPS) + n)
                    dve.scalar_tensor_tensor(out=cv_sum[1][:, back:], in0=u[:, c, 0:T - back],
                                             scalar=col("conf_dw_w", (STEPS - back) * DK + c),
                                             in1=cv_sum[1][:, back:], op0=ALU.mult, op1=ALU.add).then_inc(cv_step, 1)

            def gate(c):
                dve.wait_ge(ga_v, c + 1)
                dve.wait_ge(sg_done, c + 1)
                dve.scalar_tensor_tensor(out=u[:, c, :], in0=u[:, c, :], scalar=col("b_glu", c), in1=bank[2 + c % 2][:, :],
                                         op0=ALU.add, op1=ALU.mult).then_inc(u_done, 1)

            for i in range(DK // 2):
                for t in range(2):
                    wait_tile(dve, t, IT_GLU + i, PR_GLU + i)
                    dve.tensor_tensor(u[:, 2 * i + t, :], bank[t][:, :], rs_row[:, :], ALU.mult).then_inc(ga_v, 1)
                    conv(4 * i + t)
                if i == 0:
                    dve.wait_ge(dt_t, 1)
                    dve.tensor_tensor(dt_row[:, :], bank[6][0:HEADS, :], rs_row[0:HEADS, :], ALU.mult).then_inc(dt_scaled, 1)
                if i == 1:
                    dve.wait_ge(dt_t, 2)
                    dve.wait_ge(small_in, 64)
                    dve.tensor_tensor(dt_tok[:, :, :], bank[7][:, 0:SC * HEADS].rearrange("p (c h) -> p c h", c=SC),
                                      dtb[:, :].unsqueeze(1).to_broadcast([P, SC, HEADS]), ALU.add).then_inc(dt_v, 1)
                for t in range(2):
                    wait_tile(dve, 2 + t, IT_GLU + i, PR_GLU + i)
                    dve.tensor_tensor(bank[2 + t][:, :], bank[2 + t][:, :], rs_row[:, :], ALU.mult).then_inc(gg_v, 1)
                    if t:
                        gate(2 * i)
                    conv(4 * i + 2 + t)
                gate(2 * i + 1)
                if i == DK // 2 - 1:
                    dve.wait_ge(dt_s, 4)
                    dve.scalar_tensor_tensor(out=dt_tok[:, :, :], in0=dt_tok[:, :, :], scalar=0.0, in1=t_abs[:, :, :],
                                             op0=ALU.max, op1=ALU.add).then_inc(dt_v, 1)
                    dve.wait_ge(dt_v, 2)
                    dve.scalar_tensor_tensor(out=da_tok[:, :, :], in0=dt_tok[:, :, :], scalar=-1.0,
                                             in1=alog[:, :].unsqueeze(1).to_broadcast([P, SC, HEADS]),
                                             op0=ALU.mult, op1=ALU.mult).then_inc(dt_v, 1)
            for i in range(XT // 4):
                for b0 in (0, 2):
                    for e in range(2):
                        b = b0 + e
                        wait_tile(dve, b, IT_XBC + i, PR_XBC + i)
                        dve.tensor_tensor(bank[b][:, :], bank[b][:, :], rs_row[:, :], ALU.mult).then_inc(xs_v, 1)
                        if e == 0:
                            conv(2 * DK + 4 * i + b0)
                    for s in range(1, STAPS):
                        for e in range(2):
                            b = b0 + e
                            c = 4 * i + b
                            done = short_steps(c) - 1 - 2 * (STAPS - 1 - s)
                            if s == 1:
                                dve.wait_ge(cb_start, c + 1)
                            else:
                                dve.wait_ge(cb_step, done - 1)
                            dve.scalar_tensor_tensor(out=xbc[:, c, s:], in0=bank[b][:, 0:T - s],
                                                     scalar=col("ssd_conv_w", (STAPS - 1 - s) * XT + c),
                                                     in1=xbc[:, c, s:], op0=ALU.mult, op1=ALU.add).then_inc(cb_step, 1)
                    conv(2 * DK + 4 * i + b0 + 1)
                if i == 0:
                    dve.wait_ge(acs_t, 2)
                    dve.tensor_copy(acs[:, :, :].rearrange("p c h -> p (c h)"), bank[6][:, 0:64]).then_inc(acs_v, 1)
                    dve.wait_ge(acs_v, 1)
                    dve.tensor_tensor(wdec[:, :, :].rearrange("p c h -> p (c h)"), bank[6][:, 64:128],
                                      acs[:, :, :].rearrange("p c h -> p (c h)"), ALU.subtract).then_inc(acs_v, 1)
                    dve.wait_ge(acs_split, 2)
                    dve.tensor_tensor(acs_lo[:, :], bank[7][0:HEADS, :], acs_hi[:, :].bitcast(F32),
                                      ALU.subtract).then_inc(acs_v, 1)

            def scale_z(c):
                wait_tile(dve, c % 4, IT_Z + c // 4, PR_Z + c // 4)
                dve.tensor_tensor(bank[c % 4][:, :], bank[c % 4][:, :], rs_row[:, :], ALU.mult).then_inc(zs_v, 1)

            def heads(ap):
                return ap.rearrange("p (h d) -> p h d", d=HD)

            def dt_x(n):
                c, g = n // 2, n % 2
                dve.wait_ge(xt_t, n + 1)
                dve.tensor_tensor(heads(x_dt[:, c, g * T:(g + 1) * T]), heads(bank[6 + g][:, :]),
                                  dt_tok[:, c, g * HG:(g + 1) * HG].unsqueeze(2).to_broadcast([P, HG, HD]),
                                  ALU.mult).then_inc(xt_v, 1)

            def decay_x(n):
                c, g = n // 2, n % 2
                dve.wait_ge(xt_v, n + 1)
                if n >= 2:
                    dve.wait_ge(st_t, n - 1)
                dve.tensor_tensor(heads(x_dec[:, g, :]), heads(x_dt[:, c, g * T:(g + 1) * T]),
                                  wdec[:, c, g * HG:(g + 1) * HG].unsqueeze(2).to_broadcast([P, HG, HD]),
                                  ALU.mult).then_inc(xdec_v, 1)

            def state(n):
                c, g = n // 2, n % 2
                gs = slice(g * T, (g + 1) * T)
                dve.wait_ge(st_t, n + 1)
                if c == 0:
                    dve.tensor_copy(hst[:, 0, gs], bank[4 + g][:, :]).then_inc(st_v, 1)
                    return
                dve.wait_ge(st_v, n - 1)
                dve.tensor_tensor(heads(hst[:, c, gs]), heads(hst[:, c - 1, gs]),
                                  dend[:, c, g * HG:(g + 1) * HG].unsqueeze(2).to_broadcast([P, HG, HD]),
                                  ALU.mult).then_inc(st_m, 1)
                dve.wait_ge(st_m, n - 1)
                dve.tensor_tensor(hst[:, c, gs], hst[:, c, gs], bank[4 + g][:, :], ALU.add).then_inc(st_v, 1)

            z_part = 2 * DK + XT
            for c in range(DK):
                if c < 3:
                    scale_z(c)
                if c == 3:
                    for g in range(GROUPS):
                        dve.wait_ge(cbm_t, g + 1)
                        dve.tensor_tensor(g_mask[:, g, :, :], bank[6 + g][:, :].rearrange("p (c t) -> p c t", c=SC),
                                          tri[:, :].unsqueeze(1).to_broadcast([P, SC, P]), ALU.mult).then_inc(cbm_v, 1)
                if c >= 4:
                    dt_x(2 * c - 8)
                    dt_x(2 * c - 7)
                if c >= 3:
                    scale_z(c)
                if c == DK - 2:
                    dve.wait_ge(acs_s, 2)
                    decay_x(0)
                    decay_x(1)
                conv(z_part + c)
            dve.wait_ge(w_used, 2 * IT_OUT)
            state(0)
            state(1)
            decay_x(2)
            decay_x(3)
            state(2)
            state(3)
            decay_x(4)
            decay_x(5)

            def finish(q):
                b = 6 + q % 2
                dve.wait_ge(diag_t, q + 1)
                dve.wait_ge(off_v, q + 1)
                dve.tensor_tensor(bank[b][:, P:], bank[b][:, P:], e_t[:, q % 2, P:], ALU.add).then_inc(y_a, 1)
                dve.wait_ge(y_a, q + 1)
                dve.scalar_tensor_tensor(out=bank[b][:, :], in0=xbc[:, q, :], scalar=d_col[:, q:q + 1],
                                         in1=bank[b][:, :], op0=ALU.mult, op1=ALU.add).then_inc(y_d, 1)
                dve.wait_ge(y_d, q + 1)
                dve.wait_ge(z_done, q + 1)
                dve.tensor_tensor(z[:, q, :], z[:, q, :], bank[b][:, :], ALU.mult).then_inc(y_v, 1)

            def norm_y(g):
                dve.wait_ge(ssdn[g].row, 1)
                for k in range(DK // GROUPS * g, DK // GROUPS * (g + 1)):
                    dve.scalar_tensor_tensor(out=z[:, k, :], in0=z[:, k, :], scalar=col("ssd_norm_g", k),
                                             in1=bank[3 * g][:, :], op0=ALU.mult, op1=ALU.mult).then_inc(ssdn[g].val, 1)

            def rest_y(g, k):
                m = DK // GROUPS * g + k
                dve.wait_ge(ssdn[g].hi, k + 1)
                dve.tensor_tensor(ysl[:, m, :], z[:, m, :], ysh[:, m, :].bitcast(F32), ALU.subtract).then_inc(ssdn[g].lo, 1)

            def masked(q):
                g = q // (DK // GROUPS)
                for e in range(2):
                    h = 2 * q + e
                    dve.wait_ge(l_s, h + 1)
                    if q >= 2:
                        dve.wait_ge(diag_t, q - 1)
                    dve.tensor_tensor(m_t[:, h % 4, :], l_t[:, e, :], g_mask[:, g, :, :].rearrange("p c t -> p (c t)"),
                                      ALU.mult).then_inc(m_v, 1)

            masked(0)
            state(4)
            state(5)
            for q in range(DK):
                if q:
                    masked(q)
                dve.wait_ge(e_s, q + 1)
                dve.wait_ge(off_t, q + 1)
                dve.tensor_tensor(e_t[:, q % 2, P:], e_t[:, q % 2, P:], bank[4][:, P:], ALU.mult).then_inc(off_v, 1)
                conv_rest(q)
                if q:
                    finish(q - 1)
            invert(ssdn[0])
            finish(DK - 1)
            norm_y(0)
            invert(ssdn[1])
            for k in range(DK // GROUPS):
                rest_y(0, k)
            norm_y(1)
            for k in range(DK // GROUPS):
                rest_y(1, k)
            dve.wait_ge(mu_t, 1)
            for c in range(DK):
                dve.tensor_tensor(u[:, c, :], u[:, c, :], bank[5][:, :], ALU.add).then_inc(cen_v, 1)
            invert(lnn)
            dve.wait_ge(lnn.row, 1)
            for c in range(DK):
                dve.scalar_tensor_tensor(out=u[:, c, :], in0=u[:, c, :], scalar=col("conf_ln_g", c), in1=bank[7][:, :],
                                         op0=ALU.mult, op1=ALU.mult).then_inc(lnn.val, 1)
            for c in range(DK):
                dve.wait_ge(lnn.hi, c + 1)
                dve.tensor_tensor(ycl[:, c, :], u[:, c, :], ych[:, c, :].bitcast(F32), ALU.subtract).then_inc(lnn.lo, 1)

            add_squares(postm)
            post_norm(postm, "mix_post_g", lambda k: rest_x(pre2, "ffn2_pre_g", k))
            invert(pre2)
            keep_row(pre2)
            gate_up(1, IT_GU2, PR_GU2)
            dve.wait_ge(w_used, 2 * IT_DOWN2)
            add_squares(post2)
            for k in range(0, DK, 2):
                scale_out(post2, "ffn2_post_g", k)
                scale_out(post2, "ffn2_post_g", k + 1)
                add_out(post2, k)
            add_out(post2, DK - 1)
            for c in range(SC):
                dve.wait_ge(out_turned, SC + c + 1)
                dve.tensor_copy(x_tok[:, c, T:2 * T], bank[end_bank(1, c)][:, :]).then_inc(out_copied[1], 1)

        @block.tensor
        def _(pe):
            def three(dst, s, blk, t, hi, lo, first, last):
                c0 = blk * CW + t * P
                pe.matmul(dst, w_lo[s][:, c0:c0 + P], hi, start=first, stop=False)
                pe.matmul(dst, w_hi[s][:, c0:c0 + P], lo, start=False, stop=False)
                return pe.matmul(dst, w_hi[s][:, c0:c0 + P], hi, start=False, stop=last)

            def project(it, free, after=None):
                for s in range(2):
                    pe.wait_ge(lo_done, it * 2 + (s + 1))
                    for t in range(2):
                        for sm, v in free(2 * s + t):
                            pe.wait_ge(sm, v)
                        for k in range(DK):
                            last = three(bank[2 * s + t][:, :], s, k, t, xh[:, k, :], xl[:, k, :], k == 0, k == DK - 1)
                        last.then_inc(w_used if t else tile_done[s], 1)
                        if after:
                            after(2 * s + t)

            def sums(nm, src, b, first, last):
                for c in range(SC):
                    mm = pe.matmul(bank[b][:, c:c + 1], src[:, c * P:(c + 1) * P], ones[:, 0:1],
                                   start=(first and c == 0), stop=(last and c == SC - 1), skip_group_check=True)
                if nm:
                    mm.then_inc(nm.sum, 1)
                return mm

            def spread(src, b, done):
                for c in range(SC):
                    mm = pe.matmul(bank[b][:, c * P:(c + 1) * P], src[:, c:c + 1].to_broadcast([P, P]), ident[:, :],
                                   start=True, stop=True)
                mm.then_inc(done, 1)

            def first_project(nm, it, before=None, half=DK // 2):
                if before:
                    before(0)

                def first_blocks(tiles):
                    for b in tiles:
                        c0 = (b % 2) * P
                        pe.matmul(bank[b][:, :], w_lo[b // 2][:, c0:c0 + P], xh[:, 0, :], start=True, stop=False)
                        pe.matmul(bank[b][:, :], w_hi[b // 2][:, c0:c0 + P], xh[:, 0, :], start=False, stop=False)
                    pe.wait_ge(nm.lo, 1)
                    for b in tiles:
                        c0 = (b % 2) * P
                        pe.matmul(bank[b][:, :], w_hi[b // 2][:, c0:c0 + P], xl[:, 0, :], start=False, stop=False)

                def blocks(b, ks):
                    for k in ks:
                        last = three(bank[b][:, :], b // 2, k, b % 2, xh[:, k, :], xl[:, k, :], k == 0, k == DK - 1)
                    if ks[-1] == DK - 1:
                        last.then_inc(w_used if b % 2 else tile_done[b // 2], 1)
                pe.wait_ge(lo_done, it * 2 + 1)
                pe.wait_ge(nm.hi, 1)
                first_blocks(range(2))
                for k in range(1, half):
                    pe.wait_ge(nm.lo, k + 1)
                    for b in range(2):
                        blocks(b, [k])
                    if k == 1:
                        pe.wait_ge(lo_done, it * 2 + 2)
                        for b in range(2, 4):
                            blocks(b, [0])
                    if k >= 1:
                        for b in range(2, 4):
                            blocks(b, [k])
                for k in range(max(half, 1), DK):
                    if before:
                        before(k)
                    pe.wait_ge(nm.lo, k + 1)
                    for b in range(2):
                        blocks(b, [k])
                if half:
                    pe.wait_ge(nm.add, DK - 1)
                    sums(nm, sq_sum, 7, True, True)
                    blocks(2, list(range(half, DK)))
                else:
                    pe.wait_ge(lo_done, it * 2 + 2)
                    blocks(2, list(range(DK // 2)))
                    pe.wait_ge(nm.add, DK - 1)
                    sums(nm, sq_sum, 7, True, True)
                    blocks(2, list(range(DK // 2, DK)))
                pe.wait_ge(nm.inv, 1)
                spread(rinv, 7, nm.row)
                blocks(3, list(range(half, DK)))

            def gate_up(n, nm, it0, before=None, half=DK // 2):
                first_project(nm, it0, before, half)

                def free(i):
                    tl = i * 2 + (n * FK - 1)
                    return lambda b: [(silu_done if b < 2 else hl_done, tl + b % 2)]
                with pe.Fori(1, FK // 2) as i:
                    project(i + it0, free(i))

            def down(n, nm, it0):
                def pair(i, first):
                    for s in range(2):
                        if first:
                            for sm in (hh_done, hl_done):
                                pe.wait_ge(sm, n * FK + (s * KH + KH + 1) // 2 * 2)
                        pe.wait_ge(lo_done, i * 2 + (2 * it0 + s + 1))
                        for t in range(2):
                            if s == 0 and not first:
                                pe.wait_ge(fo_done, i * 2 + (2 * DK * n + t - 1))
                            for k in range(KH):
                                kk = s * KH + k
                                last = three(bank[4 + t][:, :], s, k, t, hh[:, kk, :], hl[:, kk, :], kk == 0, kk == FK - 1)
                            if t:
                                last.then_inc(w_used, 1)
                            elif s:
                                last.then_inc(acc_done, 1)
                pair(0, True)
                with pe.Fori(1, DK // 2) as i:
                    pair(i, False)

            def post_norm(nm):
                pe.wait_ge(nm.add, DK)
                sums(None, sq_norm, 6, True, False)
                pe.wait_ge(nm.sq, DK)
                sums(nm, sq_out, 6, False, True)
                pe.wait_ge(nm.inv, 1)
                spread(rinv, 6, nm.row)

            pe.wait_ge(consts, 5)
            pe.wait_ge(x_in, 16 * SC)

            def turn(k):
                if k >= 3:
                    pe.wait_ge(x_ready, k - 2)
                for c in range(SC):
                    mm = pe.transpose(bank[turn_bank(k)][:, c * P:(c + 1) * P], x_tok[:, c, k * P:(k + 1) * P], ident[:, :])
                mm.then_inc(x_turned, 1)

            pe.wait_ge(par_in, 16 * (len(VECS) + 3))
            at_col = 0
            for i, rows in enumerate((NVEC, STAPS * XT, HALF_ROWS, HALF_ROWS)):
                last = pe.transpose(bank[7][:, at_col:at_col + rows], par_rows[0:rows, i, :], ident[0:rows, 0:rows])
                at_col += rows
            last.then_inc(par_t, 1)
            for k in range(3):
                turn(k)

            def turn_next(k):
                if k == 0:
                    pe.wait_ge(par_ok, 2)
                if k + 3 < DK:
                    turn(k + 3)
            gate_up(0, pre1, IT_GU1, turn_next, 0)
            down(0, post1, IT_DOWN1)
            post_norm(post1)
            first_project(prem, IT_GLU)

            pe.wait_ge(dtw_lo, 1)
            for k in range(DK):
                dst = bank[6][0:HEADS, :]
                pe.matmul(dst, dtwl[:, k, :], xh[:, k, :], start=(k == 0), stop=False)
                pe.matmul(dst, dtwh[:, k, :], xl[:, k, :], start=False, stop=False)
                last = pe.matmul(dst, dtwh[:, k, :], xh[:, k, :], start=False, stop=(k == DK - 1))
            last.then_inc(dt_t, 1)

            def turn_dt(b):
                if b == 0:
                    pe.wait_ge(dt_scaled, 1)
                    for c in range(SC):
                        mm = pe.transpose(bank[7][:, c * HEADS:(c + 1) * HEADS], dt_row[:, c * P:(c + 1) * P],
                                          ident[0:HEADS, 0:HEADS])
                    mm.then_inc(dt_t, 1)

            def glu_free(i):
                return lambda b: [(ga_v, 2 * i + b + 1) if b < 2 else (u_done, 2 * i + b - 1)]
            for i in range(1, DK // 2):
                project(IT_GLU + i, glu_free(i - 1), turn_dt if i == 1 else None)

            def sum_decays(b):
                if b == 1:
                    pe.wait_ge(dt_v, 3)
                    da = da_tok[:, :, :].rearrange("p c h -> p (c h)")
                    pe.matmul(bank[6][:, 0:64], tri[:, :], da, start=True, stop=True)
                    pe.matmul(bank[6][:, 64:128], ones[:, :], da, start=True, stop=True).then_inc(acs_t, 1)
                    for c in range(SC):
                        mm = pe.matmul(bank[7][0:HEADS, c * P:(c + 1) * P], da_tok[:, c, :], tri[:, :], start=True, stop=True)
                    mm.then_inc(acs_t, 1)
            project(IT_XBC, glu_free(DK // 2 - 1), sum_decays)
            for i in range(1, XT // 4):
                project(IT_XBC + i, lambda b: [(cb_step, short_steps(4 * (i - 1) + b))])

            def turn_x(n):
                c, g = n // 2, n % 2
                if n >= 2:
                    pe.wait_ge(xt_v, n - 1)
                else:
                    pe.wait_ge(cbm_v, n + 1)
                for j in range(4):
                    last = pe.transpose(bank[6 + g][:, j * P:(j + 1) * P], xbc[:, 4 * g + j, c * P:(c + 1) * P], ident[:, :])
                last.then_inc(xt_t, 1)

            def operands(b):
                if b == 1:
                    pe.wait_ge(xbc_done, XT)
                    pe.wait_ge(acs_v, 3)
                    pe.wait_ge(acs_s, 2)
                    for g in range(GROUPS):
                        for c in range(SC):
                            last = pe.transpose(bank[6 + g][:, c * P:(c + 1) * P], xbc[:, DK + g, c * P:(c + 1) * P], ident[:, :])
                        last.then_inc(bt_t, 1)
                if b == 2:
                    for g in range(GROUPS):
                        pe.wait_ge(bt_c, g + 1)
                        for c in range(SC):
                            cs = slice(c * P, (c + 1) * P)
                            last = pe.matmul(bank[6 + g][:, cs], xbc[:, DK + g, cs], xbc[:, DK + GROUPS + g, cs],
                                             start=True, stop=True)
                        last.then_inc(cbm_t, 1)

            def turns(b):
                if b < 3:
                    turn_x(2 * b + 2)
                    turn_x(2 * b + 3)
            project(IT_Z, lambda b: [(cb_step, short_steps(XT - 4 + b))], operands)
            turn_x(0)
            turn_x(1)
            project(IT_Z + 1, lambda b: [(z_done, b + 1)], turns)

            def state(n):
                c, g = n // 2, n % 2
                pe.wait_ge(xdec_v, n + 1)
                if n >= 2:
                    pe.wait_ge(st_v, n - 1)
                else:
                    pe.wait_ge(cp_start, 3 + n)
                pe.matmul(bank[4 + g][:, :], b_tok[:, g, c, :], x_dec[:, g, :], start=True, stop=True).then_inc(st_t, 1)

            def sums_per_head(q):
                if q:
                    pe.wait_ge(seg_s, 2 * SC * q)
                else:
                    pe.wait_ge(z_done, 7)
                    pe.wait_ge(acs_split, 2)
                    pe.wait_ge(acs_v, 3)
                for e in range(2):
                    one = pick_one[:, 2 * q + e:2 * q + e + 1].to_broadcast([HEADS, P])
                    pe.matmul(bank[e][:, :], one, acs_lo[:, :], start=True, stop=False)
                    last = pe.matmul(bank[e][:, :], one, acs_hi[:, :], start=False, stop=True)
                last.then_inc(r_t, 1)

            def sums_per_tile(q):
                if q:
                    pe.wait_ge(e_s, q)
                else:
                    pe.wait_ge(acs_split, 3)
                two = pick_two[:, 2 * q:2 * q + 2, :].rearrange("k h d -> k (h d)")
                pe.matmul(bank[2][:, :], two, acs_lo[:, :], start=True, stop=False)
                pe.matmul(bank[2][:, :], two, acs_hi[:, :], start=False, stop=True).then_inc(r_t, 1)

            def off(q):
                g = q // (DK // GROUPS)
                if q:
                    pe.wait_ge(off_v, q)
                for c in range(1, SC):
                    cs = slice(c * P, (c + 1) * P)
                    last = pe.matmul(bank[4][:, cs], hst[:, c - 1, q * P:(q + 1) * P], xbc[:, DK + GROUPS + g, cs],
                                     start=True, stop=True)
                last.then_inc(off_t, 1)

            def diag(q):
                if q >= 2:
                    pe.wait_ge(y_v, q - 1)
                for e in range(2):
                    h = 2 * q + e
                    pe.wait_ge(m_v, h + 1)
                    for c in range(SC):
                        cs = slice(c * P, (c + 1) * P)
                        last = pe.matmul(bank[6 + q % 2][e * HD:(e + 1) * HD, cs], x_dt[:, c, h * HD:(h + 1) * HD],
                                         m_t[:, h % 4, cs], start=True, stop=True)
                last.then_inc(diag_t, 1)

            def sum_y(g):
                if g:
                    pe.wait_ge(ssdn[0].root, 1)
                else:
                    pe.wait_ge(z_done, DK)
                pe.wait_ge(ssdn[g].add, DK // GROUPS - 2)
                sums(None, sq_y[0], 3, True, False)
                pe.wait_ge(ssdn[g].sq, DK // GROUPS)
                sums(ssdn[g], sq_y[1], 3, False, True)

            def mean(pair, done, count, first=False, last=False):
                for e in range(2):
                    pe.wait_ge(done, count + e)
                    mm = pe.matmul(bank[5][:, :], less_mean[:, :], u[:, 2 * pair + e, :], start=first and e == 0,
                                   stop=last and e == 1)
                if last:
                    mm.then_inc(mu_t, 1)

            sums_per_head(0)
            for n in range(6):
                state(n)
                if n == 1:
                    sums_per_tile(0)
                if n == 3:
                    sums_per_head(1)
                    sums_per_tile(1)
            pe.wait_ge(st_v, 6)
            pe.wait_ge(xt_v, 2 * SC)
            for q in range(DK):
                off(q)
                if 0 < q < DK - 1:
                    sums_per_head(q + 1)
                    sums_per_tile(q + 1)
                diag(q)
                if q == DK // GROUPS + 1:
                    sum_y(0)
                if q == 1:
                    mean(DVE_JOBS[0][0], cv_out, 1, first=True)
                if q == 2:
                    mean(DVE_JOBS[1][0], cv_out, 3)
                if q == 3:
                    mean(POOL_JOBS[0][0], cp_out, 1)
            pe.wait_ge(ssdn[0].inv, 1)
            pe.wait_ge(seg_s, 2 * SC * DK)
            spread(rinv, 0, ssdn[0].row)
            sum_y(1)
            pe.wait_ge(ssdn[1].inv, 1)
            spread(rinv, 3, ssdn[1].row)
            mean(POOL_JOBS[1][0], cp_out, 3, last=True)

            def out_tile(j, t):
                half, m = OUT_CHUNKS[j]
                hi, lo = (ych, ycl) if half else (ysh, ysl)
                b = out_bank(2 * m + t)
                if t == 0:
                    pe.wait_ge(lo_done, 2 * IT_OUT + j + 1)
                if half == 0 and 2 * m + t >= 6:
                    pe.wait_ge(fo_done, DK + 2 * m + t - 6 + 1)
                for k in range(DK):
                    if j == 0 and t == 0:
                        pe.wait_ge(ssdn[k // (DK // GROUPS)].lo, k % (DK // GROUPS) + 1)
                    if j == OUT_CHUNKS.index((1, 0)) and t == 0:
                        pe.wait_ge(lnn.lo, k + 1)
                    last = three(bank[b][:, :], j % 2, k, t, hi[:, k, :], lo[:, k, :], half == 0 and k == 0,
                                 half == 1 and k == DK - 1)
                if t:
                    last.then_inc(w_used, 1)
                elif half:
                    last.then_inc(acc_done, 1)

            for j in range(len(OUT_CHUNKS)):
                out_tile(j, 0)
                if j == 1:
                    pe.wait_ge(lnn.add, DK - 1)
                    sums(lnn, sq_sum, 7, True, True)
                out_tile(j, 1)
                if j == 1:
                    pe.wait_ge(lnn.inv, 1)
                    spread(rinv, 7, lnn.row)
            post_norm(postm)
            gate_up(1, pre2, IT_GU2)
            down(1, post2, IT_DOWN2)
            post_norm(post2)
            for k in range(DK):
                h, j = k // 4, k % 4
                if k % 2 and k < DK - 1:
                    pe.wait_ge(val_pool, k // 2 + 1)
                else:
                    pe.wait_ge(post2.val, DK // 2 + 1 if k == DK - 1 else k // 2 + 1)
                for c in range(SC):
                    if k == 4 and end_bank(1, c) < SC:
                        pe.wait_ge(out_copied[0], end_bank(1, c) + 1)
                    last = pe.transpose(bank[end_bank(h, c)][:, j * P:(j + 1) * P], x[:, k, c * P:(c + 1) * P], ident[:, :])
                    if j == 3:
                        last.then_inc(out_turned, 1)


def short_steps(c):
    return (c // 2) * 2 * (STAPS - 1) + 2 * (STAPS - 2) + c % 2 + 1


_INS = ["x", "ffn1_pre_g", "ffn1_w_gate", "ffn1_w_up", "ffn1_w_down", "ffn1_post_g", "mix_pre_g", "w_in", "b_glu",
        "ssd_conv_w", "ssd_conv_b", "dt_bias", "a_log", "d_skip", "ssd_norm_g", "conf_dw_w", "conf_dw_b",
        "conf_ln_g", "conf_ln_b", "w_out", "mix_post_g", "ffn2_pre_g", "ffn2_w_gate", "ffn2_w_up", "ffn2_w_down",
        "ffn2_post_g"]


def kernel(**inputs):
    import numpy as _np
    import concourse.bacc as _bacc
    from concourse import mybir as _mybir
    from concourse.bass_utils import run_bass_kernel_spmd as _run

    nc = _bacc.Bacc("TRN2", target_bir_lowering=False, num_devices=1)
    arrays, args = {}, {}
    for name in _INS:
        arr = _np.ascontiguousarray(inputs[name])
        arrays[f"in_{name}"] = arr
        args[name] = nc.dram_tensor(f"in_{name}", arr.shape, _mybir.dt.from_np(arr.dtype), kind="ExternalInput").ap()
    out = nc.dram_tensor("out_x", (1, T, D), F32, kind="ExternalOutput").ap()
    build(nc, args, out)
    r = _run(nc, [arrays], core_ids=[0])
    return r.results[0]["out_x"]
```
